# Optimizing a Trainium2 kernel written in Bass

```python
import jax, jax.numpy as jnp
from jax import lax
import numpy as np

D_MODEL = 1024
BATCH = 1
SEQ = 256
DEPTH = 1

HEAD_DIM = 64
N_Q_HEADS = D_MODEL // HEAD_DIM
N_KV_HEADS = N_Q_HEADS // 4
Q_PER_KV = N_Q_HEADS // N_KV_HEADS
ATTN_WIDTH = N_Q_HEADS * HEAD_DIM
KV_WIDTH = N_KV_HEADS * HEAD_DIM
WINDOW = 128
ATTN_BLOCK = 128
ROPE_THETA = 10000.0

CONV_WIDTH = D_MODEL
CONV_KERNEL = 3

N_BRANCH = 2
IN_WIDTH = ATTN_WIDTH + 2 * KV_WIDTH + 3 * CONV_WIDTH + N_BRANCH * D_MODEL

N_EXPERTS = 32
TOP_K = 4
D_FF = D_MODEL
SWIGLU_LIMIT = 7.0
SWIGLU_ALPHA = 1.702
MOE_BLOCK = 128

RMS_EPS = 1e-5

kernel_name = "hybrid_swa_shortconv_moe_block"

def rms_norm(x, g):
    xf = x.astype(jnp.float32)
    y = xf * lax.rsqrt(jnp.mean(xf * xf, axis=-1, keepdims=True) + RMS_EPS)
    return (y * g.astype(jnp.float32)).astype(x.dtype)

def split_points():
    widths = [ATTN_WIDTH, KV_WIDTH, KV_WIDTH, CONV_WIDTH, CONV_WIDTH, CONV_WIDTH, D_MODEL]
    pts, acc = [], 0
    for w in widths:
        acc += w
        pts.append(acc)
    return pts

def apply_rope(t, positions):
    half = HEAD_DIM // 2
    inv_freq = ROPE_THETA ** (-jnp.arange(half, dtype=jnp.float32) / half)
    ang = positions.astype(jnp.float32)[:, None] * inv_freq[None, :]
    cos = jnp.cos(ang)[None, :, None, :]
    sin = jnp.sin(ang)[None, :, None, :]
    t1 = t[..., :half].astype(jnp.float32)
    t2 = t[..., half:].astype(jnp.float32)
    out = jnp.concatenate([t1 * cos - t2 * sin, t2 * cos + t1 * sin], axis=-1)
    return out.astype(t.dtype)

def sliding_window_attention(q, k, v, sinks):
    B, S = q.shape[0], q.shape[1]
    nb = S // ATTN_BLOCK
    qb = q.reshape(B, nb, ATTN_BLOCK, N_KV_HEADS, Q_PER_KV, HEAD_DIM)

    def band(t):
        tp = jnp.pad(t, ((0, 0), (ATTN_BLOCK, 0), (0, 0), (0, 0)))
        tp = tp.reshape(B, nb + 1, ATTN_BLOCK, N_KV_HEADS, HEAD_DIM)
        return jnp.concatenate([tp[:, :-1], tp[:, 1:]], axis=2)

    kb, vb = band(k), band(v)
    scores = jnp.einsum('bnqkgd,bnskd->bnkgqs', qb, kb,
                        preferred_element_type=jnp.float32) * (HEAD_DIM ** -0.5)
    qi = jnp.arange(ATTN_BLOCK)[:, None]
    sj = jnp.arange(2 * ATTN_BLOCK)[None, :]
    dist = qi + ATTN_BLOCK - sj
    key_pos = jnp.arange(nb)[:, None, None] * ATTN_BLOCK - ATTN_BLOCK + sj[None]
    mask = (dist >= 0) & (dist < WINDOW) & (key_pos >= 0)
    scores = jnp.where(mask[None, :, None, None], scores, -jnp.inf)
    sink = sinks.astype(jnp.float32).reshape(N_KV_HEADS, Q_PER_KV)[None, None, :, :, None]
    m = jnp.maximum(scores.max(axis=-1), sink)
    p = jnp.exp(scores - m[..., None])
    denom = p.sum(axis=-1) + jnp.exp(sink - m)
    probs = (p / denom[..., None]).astype(v.dtype)
    out = jnp.einsum('bnkgqs,bnskd->bnqkgd', probs, vb)
    return out.reshape(B, S, ATTN_WIDTH)

def causal_short_conv(u, w):
    S = u.shape[1]
    up = jnp.pad(u, ((0, 0), (CONV_KERNEL - 1, 0), (0, 0)))
    y = w[0] * up[:, 0:S]
    for j in range(1, CONV_KERNEL):
        y = y + w[j] * up[:, j:j + S]
    return y

def moe_ffn(h, w_router, b_router, w_gate, b_gate, w_up, b_up, w_down, b_down):
    B, S, D = h.shape
    T = B * S
    xt = h.reshape(T, D)
    logits = (xt @ w_router).astype(jnp.float32) + b_router.astype(jnp.float32)
    top_logit, top_idx = lax.top_k(logits, TOP_K)
    top_w = jax.nn.softmax(top_logit, axis=-1).astype(h.dtype)
    A = T * TOP_K
    flat_e = top_idx.reshape(A)
    flat_tok = jnp.repeat(jnp.arange(T, dtype=jnp.int32), TOP_K)
    flat_w = top_w.reshape(A)
    order = jnp.argsort(flat_e)
    se, stok, sw = flat_e[order], flat_tok[order], flat_w[order]
    counts = jnp.bincount(flat_e, length=N_EXPERTS)
    padded = (counts + MOE_BLOCK - 1) // MOE_BLOCK * MOE_BLOCK
    start = jnp.cumsum(counts) - counts
    pad_end = jnp.cumsum(padded)
    pad_start = pad_end - padded
    dest = pad_start[se] + jnp.arange(A) - start[se]
    n_blocks = (A + MOE_BLOCK - 1) // MOE_BLOCK + N_EXPERTS
    P = n_blocks * MOE_BLOCK
    buf_tok = jnp.full((P,), T, jnp.int32).at[dest].set(stok)
    buf_w = jnp.zeros((P,), h.dtype).at[dest].set(sw)
    blk_e = jnp.minimum(
        jnp.searchsorted(pad_end, jnp.arange(n_blocks) * MOE_BLOCK, side='right'),
        N_EXPERTS - 1)
    x_pad = jnp.concatenate([xt, jnp.zeros((1, D), xt.dtype)], axis=0)
    xb = x_pad[buf_tok].reshape(n_blocks, MOE_BLOCK, D)

    def expert_block(args):
        xblk, e = args
        g = xblk @ w_gate[e] + b_gate[e]
        u = xblk @ w_up[e] + b_up[e]
        g = jnp.minimum(g, SWIGLU_LIMIT)
        u = jnp.clip(u, -SWIGLU_LIMIT, SWIGLU_LIMIT)
        a = g * jax.nn.sigmoid(SWIGLU_ALPHA * g) * (u + 1.0)
        return a @ w_down[e] + b_down[e]

    yb = lax.map(expert_block, (xb, blk_e))
    y = jnp.zeros((T + 1, D), h.dtype).at[buf_tok].add(yb.reshape(P, D) * buf_w[:, None])
    return y[:T].reshape(B, S, D)

def setup_inputs(seed: int = 0) -> dict:
    key = jax.random.key(seed)
    ks = jax.random.split(key, 20)
    f32 = jnp.float32
    nrm = lambda k, shape, s: jax.random.normal(k, shape, f32) * s
    L = DEPTH
    return {
        "x": nrm(ks[0], (BATCH, SEQ, D_MODEL), 1.0),
        "g_mix": 1.0 + nrm(ks[1], (L, D_MODEL), 0.02),
        "w_in": nrm(ks[2], (L, D_MODEL, IN_WIDTH), D_MODEL ** -0.5),
        "b_in": nrm(ks[3], (L, IN_WIDTH), 0.02),
        "sinks": nrm(ks[4], (L, N_Q_HEADS), 0.5),
        "w_conv": nrm(ks[5], (L, CONV_KERNEL, CONV_WIDTH), CONV_KERNEL ** -0.5),
        "w_attn_o": nrm(ks[6], (L, ATTN_WIDTH, D_MODEL), ATTN_WIDTH ** -0.5),
        "w_conv_o": nrm(ks[7], (L, CONV_WIDTH, D_MODEL), CONV_WIDTH ** -0.5),
        "w_out": nrm(ks[8], (L, D_MODEL, D_MODEL), D_MODEL ** -0.5),
        "g_ffn": 1.0 + nrm(ks[9], (L, D_MODEL), 0.02),
        "w_router": nrm(ks[10], (L, D_MODEL, N_EXPERTS), D_MODEL ** -0.5),
        "b_router": nrm(ks[11], (L, N_EXPERTS), 0.01),
        "w_gate": nrm(ks[12], (L, N_EXPERTS, D_MODEL, D_FF), D_MODEL ** -0.5),
        "b_gate": nrm(ks[13], (L, N_EXPERTS, D_FF), 0.02),
        "w_up": nrm(ks[14], (L, N_EXPERTS, D_MODEL, D_FF), D_MODEL ** -0.5),
        "b_up": nrm(ks[15], (L, N_EXPERTS, D_FF), 0.02),
        "w_down": nrm(ks[16], (L, N_EXPERTS, D_FF, D_MODEL), D_FF ** -0.5),
        "b_down": nrm(ks[17], (L, N_EXPERTS, D_MODEL), 0.02),
        "g_final": 1.0 + nrm(ks[18], (D_MODEL,), 0.02),
    }

def reference(x, g_mix, w_in, b_in, sinks, w_conv, w_attn_o, w_conv_o, w_out, g_ffn,
              w_router, b_router, w_gate, b_gate, w_up, b_up, w_down, b_down, g_final):
    B, S = x.shape[0], x.shape[1]
    positions = jnp.arange(S, dtype=jnp.int32)
    pts = split_points()
    for layer in range(DEPTH):
        h = rms_norm(x, g_mix[layer])
        proj = h @ w_in[layer] + b_in[layer]
        q, k, v, cb, cc, cx, ga, gc = jnp.split(proj, pts, axis=-1)
        q = apply_rope(q.reshape(B, S, N_Q_HEADS, HEAD_DIM), positions)
        k = apply_rope(k.reshape(B, S, N_KV_HEADS, HEAD_DIM), positions)
        v = v.reshape(B, S, N_KV_HEADS, HEAD_DIM)
        y_attn = sliding_window_attention(q, k, v, sinks[layer]) @ w_attn_o[layer]
        y_conv = (cb * causal_short_conv(cc * cx, w_conv[layer])) @ w_conv_o[layer]
        merged = jax.nn.sigmoid(ga) * y_attn + jax.nn.sigmoid(gc) * y_conv
        x = x + merged @ w_out[layer]
        h = rms_norm(x, g_ffn[layer])
        x = x + moe_ffn(h, w_router[layer], b_router[layer], w_gate[layer], b_gate[layer],
                        w_up[layer], b_up[layer], w_down[layer], b_down[layer])
    return rms_norm(x, g_final)


_drawn_inputs = setup_inputs


def setup_inputs(seed=0):
    import zlib

    import numpy as np

    out = dict(_drawn_inputs(seed))
    spreads = {}
    factors = {'sinks': 4.911, 'b_gate': 6.776, 'b_up': 8.0, 'b_down': 6.53, 'g_final': 2.902}
    for name, (base, spread) in spreads.items():
        noise = np.random.default_rng([zlib.crc32(name.encode()), seed]).standard_normal(out[name].shape)
        drawn = base * np.exp(spread * noise) if base else spread * noise
        out[name] = __import__('jax').numpy.asarray(drawn.astype(out[name].dtype))
    for name, factor in factors.items():
        out[name] = (out[name] * factor).astype(out[name].dtype)
    return out
```

```python
from contextlib import ExitStack

import concourse.bass as bass
import numpy as np
from concourse import mybir

F32 = mybir.dt.float32
BF16 = mybir.dt.bfloat16
I32 = mybir.dt.int32
U32 = mybir.dt.uint32
ALU = mybir.AluOpType
ACT = mybir.ActivationFunctionType
AX = mybir.AxisListType

P = 128
D = 1024
KB = D // P
T = 256
TT = T // P
HD = 64
NQ = D // HD
NKV = NQ // 4
NE = 32
TOPK = 4
EPS = 1e-5
LIMIT, ALPHA = 7.0, 1.702
CW = 64
CAP = 64
NJ = T * TOPK // CAP - 1
NK = T // CAP - 1
NEVER = 999.0
MASKED = -3.0e38

PW = 256
NIN = 6 * NKV + 2
NP1 = NIN + 12
RING1 = 6
RING = 16
EP = 12
UNROLL = 4
assert EP * UNROLL % RING == 0 and NE % UNROLL == 0

C_ID, C_TRI, C_ONE, C_M0, C_M1 = 0, 128, 256, 384, 512
C_IOTA = 768
C_COS, C_SIN = 832, 1088
C_COL = 1344
C_UP = 1346
C_W = 1410


def shape_constants():
    c = np.zeros((P, C_W), np.float32)
    p = np.arange(P)
    c[:, C_ID:C_ID + P] = np.eye(P)
    c[:, C_TRI:C_TRI + P] = p[:, None] < p[None, :]
    c[:, C_ONE:C_ONE + P] = 1.0
    c[:, C_M0:C_M0 + P] = np.where(p[None, :] <= p[:, None], 0.0, MASKED)
    dist = p[:, None] + P - np.arange(2 * P)[None, :]
    c[:, C_M1:C_M1 + 2 * P] = np.where((dist >= 0) & (dist < P), 0.0, MASKED)
    c[:, C_IOTA:C_IOTA + CW] = np.where(np.arange(CW) < CAP, np.arange(CW), -1)
    half = HD // 2
    inv = np.float32(10000.0) ** (-np.arange(half, dtype=np.float32) / np.float32(half))
    ang = np.arange(T, dtype=np.float32)[None, :] * inv[p % half][:, None]
    c[:, C_COS:C_COS + T] = np.cos(ang)
    c[:, C_SIN:C_SIN + T] = np.sin(ang) * np.where(p % HD < half, -1.0, 1.0)[:, None]
    c[:, C_COL] = p
    c[:, C_UP:C_UP + CW] = np.arange(CW)
    c[:, C_COL + 1] = -0.5
    return c


class Steps:

    def __init__(self, eng, sem):
        self.eng, self.sem, self.n, self.base = eng, sem, 0, 0

    def link(self, ins):
        ins.then_inc(self.sem, 1)
        self.n += 1
        self.eng.wait_ge(self.sem, self.base + self.n)

    def begin_loop(self, i, per_turn):
        self.at, self.per_turn, self.before = self.n, per_turn, self.base
        self.base = self.before + i * per_turn

    def end_loop(self, turns):
        assert self.n - self.at == self.per_turn, (self.n - self.at, self.per_turn)
        self.base = self.before
        self.n = self.at + self.per_turn * turns


def hybrid_block(nc, A, out):
    ctx = ExitStack()
    with ctx:
        def sb(name, shape, dt=F32):
            return ctx.enter_context(nc.sbuf_tensor(name, shape, dt))

        def sem(name):
            return ctx.enter_context(nc.semaphore(name))

        ring = sb("ring", [P, RING, KB * PW])
        cst = sb("cst", [P, C_W])
        xres = sb("xres", [P, TT, D])
        normed = sb("normed", [P, TT, D])
        h2b = sb("h2b", [P, 3, TT, D], BF16)
        mt = sb("mt", [P, KB, T])
        gbc = sb("gbc", [P, D])
        wr = sb("wr", [P, KB, NE])
        brow = sb("brow", [33, 2 * D])
        work = sb("work", [P, 5120])
        params = sb("params", [84, P])
        parT = sb("parT", [P, 84])
        snk = sb("snk", [P, NQ])
        brt = sb("brt", [P, NE])
        small = sb("small", [P, 64])
        G = sb("G", [P, TT, CW], BF16)
        tri16 = sb("tri16", [P, 2 * P], BF16)
        pos = sb("pos", [P, TT, NE + 1])
        wgt = sb("wgt", [P, TT, NE + 1])
        Mf = sb("Mf", [P, TT, NE])
        Mb = sb("Mb", [P, TT, NE], BF16)
        cnt = sb("cnt", [P, NE])
        novt = sb("novt", [P, 1], I32)
        psum = ctx.enter_context(nc.psum_tensor("psum", [P, 8, 512], F32))

        def slot(s):
            return ring[:, s, :]
        hT = slot(6).rearrange("p (k t) -> p k t", k=KB)
        ga = slot(8).rearrange("p (k t) -> p k t", k=KB)
        gc = slot(9).rearrange("p (k t) -> p k t", k=KB)
        zT = slot(10).rearrange("p (k t) -> p k t", k=KB)
        attnT = slot(12).rearrange("p (k t) -> p k t", k=KB)
        kT = slot(14)[:, 0:512].rearrange("p (b t) -> p b t", b=2)
        V = slot(14)[:, 512:1024].rearrange("p (a c) -> p a c", a=TT)
        vcur = slot(14)[:, 1024:1152].rearrange("p (a c) -> p a c", a=TT)
        q = slot(14)[:, 1152:1664].rearrange("p (b t) -> p b t", b=2)
        kz = slot(15).rearrange("p (g h t) -> p g h t", g=NKV, h=2)
        sm = work[:, 0:1536]
        pT = work[:, 1536:3072].rearrange("p (n q) -> p n q", q=P)
        raw = work[:, 3072:3584].rearrange("p (b t) -> p b t", b=2)
        swp = work[:, 3584:4096].rearrange("p (b t) -> p b t", b=2)
        ccs = slot(11)[:, 0:512].rearrange("p (b t) -> p b t", b=2)
        u = work[:, 4096:4096 + 2 * (T + 2)].rearrange("p (b t) -> p b t", b=2)
        ycv = slot(13)[:, 0:512].rearrange("p (b t) -> p b t", b=2)
        Gw = work[:, 0:256].rearrange("p (t h c) -> p t h c", t=TT, h=2)
        S = work[:, 256:512]
        xe = work[:, 512:1024].rearrange("p (k c) -> p k c", k=KB)
        gm = work[:, 1024:1536]
        sg = work[:, 1536:2048]
        uc = work[:, 2048:2560]
        act = work[:, 2560:3072]
        aT = work[:, 3072:3584].rearrange("p (k c) -> p k c", k=KB)
        bdn = work[0:NE, 2560:3584]
        ysb = work[:, 3584:4096]
        onehot = work[:, 4096:4352].rearrange("p (t k e) -> p t k e", t=TT, k=TOPK)
        lg = work[:, 4352:4416].rearrange("p (t e) -> p t e", t=TT)
        top8 = work[:, 4416:4432].rearrange("p (t k) -> p t k", t=TT)
        topf = work[:, 4432:4448].rearrange("p (t k) -> p t k", t=TT)
        topw = work[:, 4448:4456].rearrange("p (t k) -> p t k", t=TT)
        tops = work[:, 4456:4458]
        topi = sb("topi", [P, TT, 8], U32)
        more = work[:, 4608:4608 + NK * NE]
        bv = slot(7)[:, 0:PW]
        wT = sb("wT", [NE, T])
        posT = work[0:NE, 4096:4096 + T]
        ovF = work[0:NE, 4360:4360 + NK]
        ovn, ovo = work[0:NE, 4372:4373], work[0:NE, 4373:4374]
        ovE, ovK, ovR = (work[0:NE, 4380 + n * NJ:4380 + (n + 1) * NJ] for n in range(3))
        posO = work[:, 4608:4608 + TT * NJ].rearrange("p (t j) -> p t j", t=TT)
        wgtO = work[:, 4608 + 2 * NJ:4608 + 4 * NJ].rearrange("p (t j) -> p t j", t=TT)
        eid = sb("eid", [1, NJ], I32)

        ident, tri, ones = cst[:, C_ID:C_ID + P], cst[:, C_TRI:C_TRI + P], cst[:, C_ONE:C_ONE + P]
        iota = cst[:, C_IOTA:C_IOTA + CW]
        count_up = cst[:, C_UP:C_UP + CW]
        g1T, bT, wcT = parT[:, 0:8], parT[:, 8:60], parT[:, 60:84]

        slot_full = [sem(f"slot_full{s}") for s in range(RING)]
        weights_used = sem("weights_used")
        x_in, par_in, cst_in, small_in = sem("x_in"), sem("par_in"), sem("cst_in"), sem("small_in")
        bias_full = [sem("bias_full0"), sem("bias_full1")]
        dve_step, act_step, pool_step = sem("dve_step"), sem("act_step"), sem("pool_step")
        ssq_ready, ms_ready, rstd_ready, normed_ready = (sem("ssq_ready"), sem("ms_ready"), sem("rstd_ready"),
                                                         sem("normed_ready"))
        par_turned, par_ready, x_turned, hT_ready = sem("par_turned"), sem("par_ready"), sem("x_turned"), sem("hT_ready")
        piece_done = sem("piece_done")
        raw_ready, kz_ready = sem("raw_ready"), sem("kz_ready")
        rotated = sem("rotated")
        bank6_read = sem("bank6_read")
        cc_ready, u_ready, vcur_ready = sem("cc_ready"), sem("u_ready"), sem("vcur_ready")
        z_ready, gates_ready = sem("z_ready"), sem("gates_ready")
        scores_ready, max_ready, p_ready, exp_ready = (sem("scores_ready"), sem("max_ready"), sem("p_ready"),
                                                       sem("exp_ready"))
        pT_turned, pT_ready, o_ready = sem("pT_turned"), sem("pT_ready"), sem("o_ready")
        branch_read, merged_ready, x1_ready = sem("branch_read"), sem("merged_ready"), sem("x1_ready")
        h2T_turned, h2T_ready, logits_ready = sem("h2T_turned"), sem("h2T_ready"), sem("logits_ready")
        part_ready, rest_ready = sem("part_ready"), sem("rest_ready")
        shifted_ready, topexp_ready, M_ready, ranks_ready = (sem("shifted_ready"), sem("topexp_ready"),
                                                             sem("M_ready"), sem("ranks_ready"))
        nov_ready, wgt_ready, wT_turned, wT_ready = (sem("nov_ready"), sem("wgt_ready"), sem("wT_turned"),
                                                     sem("wT_ready"))
        G_ready, Gw_ready, gathered, xe_ready = sem("G_ready"), sem("Gw_ready"), sem("gathered"), sem("xe_ready")
        gmin_ready, sig_ready, act_ready = sem("gmin_ready"), sem("sig_ready"), sem("act_ready")
        act_turned, aT_ready, S_turned, S_ready, ysb_ready, scattered = (
            sem("act_turned"), sem("aT_ready"), sem("S_turned"), sem("S_ready"), sem("ysb_ready"), sem("scattered"))
        ov_pe, ov_dve = sem("ov_pe"), sem("ov_dve")
        bdn_in = sem("bdn_in")
        gfin_in, x2_ready, out_ready, out_done = sem("gfin_in"), sem("x2_ready"), sem("out_ready"), sem("out_done")

        def pieces(w):
            return w.rearrange("(k p) n -> p k n", p=P)
        w_in, w_ao, w_co, w_o = (pieces(A[n][0]) for n in ("w_in", "w_attn_o", "w_conv_o", "w_out"))
        experts = [A[n].rearrange("l e (k p) n -> (l e) p k n", p=P) for n in ("w_up", "w_gate", "w_down")]
        KCOL, VCOL = D // PW, D // PW + 1
        first = (D + 512) // PW
        CB, CC, CX, GA, GC = (first + 4 * n for n in range(5))
        body_cols = [0, CC, CX, CB, GA, GC]

        def phys(r):
            return (r + RING1) % RING

        def uses1(s):
            return len([n for n in range(NP1) if n % RING1 == s]) if s < RING1 else 0

        block = ctx.enter_context(nc.Block())

        @block.sync
        def _(sp):
            def load1(s, src):
                sp.dma_start(ring[:, s, :].rearrange("p (k n) -> p k n", k=KB), src).then_inc(slot_full[s], 16)

            sp.dma_start(xres[:, :, :], A["x"][0].rearrange("(t p) d -> p t d", p=P)).then_inc(x_in, 16)
            load1(0, w_in[:, :, KCOL * PW:(KCOL + 1) * PW])
            load1(1, w_in[:, :, VCOL * PW:(VCOL + 1) * PW])
            for c in range(RING1 - 2):
                load1(2 + c, w_in[:, :, body_cols[c] * PW:(body_cols[c] + 1) * PW])

            ahead = [(0, 4), (0, 5), (1, 0), (1, 1), (1, 2), (1, 3)]
            with sp.Fori(0, NKV - 1) as i:
                for s, (later, c) in enumerate(ahead):
                    sp.wait_ge(piece_done, i * RING1 + (s + 1))
                    load1(s, w_in[:, :, bass.ds(i * PW + (body_cols[c] + later) * PW, PW)])
            n = NIN - 2
            tail = [w_in[:, :, (body_cols[c] + NKV - 1) * PW:(body_cols[c] + NKV) * PW] for c in (4, 5)]
            tail += [w[:, :, i * PW:(i + 1) * PW] for i in range(NKV) for w in (w_co, w_ao)]
            tail += [w_o[:, :, i * PW:(i + 1) * PW] for i in range(NKV)]
            for src in tail:
                sp.wait_ge(piece_done, n + 1 - RING1)
                load1(n % RING1, src)
                n += 1

            def load_bias(e, par):
                for m, name in enumerate(("b_up", "b_gate")):
                    sp.dma_start(brow[32 * par:32 * par + 1, m * D:(m + 1) * D],
                                 A[name][0, bass.ds(e, 1), :]).then_inc(bias_full[par], 16)

            def load_expert(e, c, wait):
                for r in range(EP):
                    s = phys((c * EP + r) % RING)
                    wait(r, s)
                    k = 2 * (r % 4)
                    sp.dma_start(ring[:, s, :].rearrange("p (k n) -> p k n", k=2),
                                 experts[r // 4][bass.ds(e, 1), :, k:k + 2, :].rearrange("a p k n -> p (a k) n"),
                                 ).then_inc(slot_full[s], 16)

            def expert_turn(it, first):
                for c in range(UNROLL):
                    if not (first and c < 2):
                        sp.wait_ge(weights_used, it * (UNROLL * EP) + ((c - 2) * EP + 8))
                    load_bias(it * UNROLL + c, c % 2)

                    def wait(r, s):
                        p = c * EP + r
                        if not (first and p < RING):
                            sp.wait_ge(weights_used, it * (UNROLL * EP) + (p + 1 - RING))
                        elif s >= RING1:
                            sp.wait_ge(piece_done, NIN + 2 * NKV)
                            sp.wait_ge(merged_ready, NKV)
                        else:
                            sp.wait_ge(piece_done, max(n for n in range(NP1) if n % RING1 == s) + 1)
                    load_expert(it * UNROLL + c, c, wait)

            expert_turn(0, True)
            with sp.Fori(1, NE // UNROLL) as it:
                expert_turn(it, False)

            sp.wait_ge(nov_ready, 1)
            nov = sp.value_load(novt[0:1, 0:1], min_val=0, max_val=NJ)
            with sp.If(nov > 0):
                sp.wait_ge(ov_dve, 3)
                with sp.Fori(0, nov) as j:
                    sp.wait_ge(scattered, j + (NE + 1))
                    e = sp.value_load(eid[0:1, bass.ds(j, 1)], min_val=0, max_val=NE - 1)
                    load_bias(e, 0)
                    load_expert(e, 0, lambda r, s: None)
            sp.wait_ge(out_ready, 2)
            sp.dma_start(out[0].rearrange("(t p) d -> p t d", p=P), normed[:, :, :]).then_inc(out_done, 16)
            sp.wait_ge(out_done, 16)

        @block.tensor
        def _(pe):
            def bank(b, lo=0, n=512):
                return psum[:, b, lo:lo + n]

            def project_T(b, s, src):
                w = ring[:, s, :].rearrange("p (k n) -> p k n", k=KB)
                for m in range(2):
                    for k in range(KB):
                        mm = pe.matmul(bank(b, m * T, T), w[:, k, m * P:(m + 1) * P], src[:, k, :],
                                       start=(k == 0), stop=(k == KB - 1))
                mm.then_inc(piece_done, 1)

            def project(b, s, src):
                w = ring[:, s, :].rearrange("p (k n) -> p k n", k=KB)
                for t in range(TT):
                    for k in range(KB):
                        mm = pe.matmul(bank(b, t * PW, PW), src[:, k, t * P:(t + 1) * P], w[:, k, :],
                                       start=(k == 0), stop=(k == KB - 1))
                mm.then_inc(piece_done, 1)

            def turn_normed(done):
                for k in range(KB):
                    for t in range(TT):
                        tr = pe.transpose(bank(3 + k // 2, (k % 2) * T + t * P, P), normed[:, t, k * P:(k + 1) * P], ident)
                    if k % 2:
                        tr.then_inc(done, 1)

            pe.wait_ge(cst_in, 16)
            pe.wait_ge(par_in, 48)
            pe.transpose(bank(7, 0, 84), params[:, :], ident[0:84, 0:84]).then_inc(par_turned, 1)
            pe.wait_ge(normed_ready, 2)
            turn_normed(x_turned)

            pe.wait_ge(par_ready, 1)
            pe.wait_ge(hT_ready, KB)
            pe.wait_ge(slot_full[0], 16)
            project_T(7, 0, hT)
            pe.wait_ge(slot_full[1], 16)
            project(6, 1, hT)
            with pe.Fori(0, NKV) as i:
                pe.wait_ge(slot_full[2], i * 16 + 16)
                project_T(2, 2, hT)
                pe.wait_ge(slot_full[3], i * 16 + 16)
                project_T(0, 3, hT)
                pe.wait_ge(rotated, i + 2)
                pe.wait_ge(kz_ready, 9)
                for m in range(2):
                    pe.matmul(psum[:, 3, m * 256:(m + 1) * 256].rearrange("p (h s) -> p h s", h=2), q[:, m, 0:P],
                              kz[:, bass.ds(i, 1), :, 0:P].rearrange("p a h s -> p (a h) s"), start=True, stop=True)
                for m in range(2):
                    mm = pe.matmul(psum[:, 4 + m, :].rearrange("p (h s) -> p h s", h=2), q[:, m, P:2 * P],
                                   kz[:, bass.ds(i, 1), :, :].rearrange("p a h s -> p (a h) s"), start=True, stop=True)
                mm.then_inc(scores_ready, 1)
                pe.wait_ge(slot_full[4], i * 16 + 16)
                project_T(1, 4, hT)
                pe.wait_ge(raw_ready, i + 2)
                pe.wait_ge(slot_full[5], i * 16 + 16)
                project_T(2, 5, hT)
                pe.wait_ge(cc_ready, i + 1)
                pe.wait_ge(slot_full[0], i * 16 + 32)
                project_T(0, 0, hT)
                pe.wait_ge(p_ready, i + 1)
                for h in range(4):
                    pe.transpose(bank(3, h * P, P), sm[:, h * P:(h + 1) * P], ident)
                for n in range(8):
                    tr = pe.transpose(bank(4 + n // 4, (n % 4) * P, P), sm[:, 512 + n * P:512 + (n + 1) * P], ident)
                tr.then_inc(pT_turned, 1)
                pe.wait_ge(u_ready, i + 1)
                pe.wait_ge(slot_full[1], i * 16 + 32)
                project_T(1, 1, hT)
                pe.wait_ge(vcur_ready, i + 1)
                pe.wait_ge(pT_ready, i * 2 + 2)
                pe.wait_ge(bank6_read, i + 1)
                o = psum[:, 6, :].rearrange("p (m t s) -> p m t s", m=2, t=TT)
                for h in range(2):
                    pe.matmul(o[64 * h:64 * h + 64, :, 0, :], vcur[:, 0, :], pT[:, h:4:2, :], start=True, stop=True,
                              tile_position=(0, 64 * h))
                for kb in range(2):
                    for h in range(2):
                        mm = pe.matmul(o[64 * h:64 * h + 64, :, 1, :], vcur[:, kb, :],
                                       pT[:, 4 + 2 * h + kb:4 + 2 * h + kb + 5:4, :], start=(kb == 0), stop=(kb == 1),
                                       tile_position=(0, 64 * h))
                mm.then_inc(o_ready, 1)
                pe.wait_ge(z_ready, i + 1)
                pe.wait_ge(gates_ready, i * 2 + 2)

            n = NIN
            for i in range(NKV):
                for src in (zT, attnT):
                    if n >= NIN + 3:
                        pe.wait_ge(branch_read, n - NIN - 2)
                    if src is attnT and i == 0:
                        pe.wait_ge(bank6_read, NKV + 1)
                    pe.wait_ge(slot_full[n % RING1], 16 * (n // RING1 + 1))
                    project_T(n % 3, n % RING1, src)
                    n += 1
            pe.wait_ge(merged_ready, NKV)
            for i in range(NKV):
                if i == 3:
                    pe.wait_ge(x1_ready, 1)
                pe.wait_ge(slot_full[n % RING1], 16 * (n // RING1 + 1))
                project(n % 3, n % RING1, mt)
                n += 1

            pe.wait_ge(normed_ready, 4)
            turn_normed(h2T_turned)
            pe.wait_ge(small_in, 16 * 5)
            pe.wait_ge(h2T_ready, 4)
            for t in range(TT):
                for k in range(KB):
                    mm = pe.matmul(bank(7, t * NE, NE), mt[:, k, t * P:(t + 1) * P], wr[:, k, :],
                                   start=(k == 0), stop=(k == KB - 1))
            mm.then_inc(logits_ready, 1)
            pe.wait_ge(M_ready, 1)
            one16, tr16 = tri16[:, P:2 * P], tri16[:, 0:P]
            pe.matmul(bank(7, 64, NE), tr16, Mb[:, 0, :], start=True, stop=True)
            pe.matmul(bank(7, 96, NE), one16, Mb[:, 0, :], start=True, stop=False)
            pe.matmul(bank(7, 96, NE), tr16, Mb[:, 1, :], start=False, stop=True)
            pe.matmul(bank(7, 128, NE), one16, Mb[:, 0, :], start=True, stop=False)
            pe.matmul(bank(7, 128, NE), one16, Mb[:, 1, :], start=False, stop=True).then_inc(ranks_ready, 1)

            def gather(nth):
                pe.wait_ge(G_ready, nth + 1)
                for k in range(KB):
                    for t in range(TT):
                        for part in range(3):
                            mm = pe.matmul(bank(6, k * CW, CW), h2b[:, part, t, k * P:(k + 1) * P], G[:, t, :],
                                           start=(t == 0 and part == 0), stop=(t == TT - 1 and part == 2))
                mm.then_inc(gathered, 1)

            def wide(b, src, c, first_r, uses, bias):
                if bias is not None:
                    par, m = bias
                    for h in range(2):
                        pe.matmul(psum[64 * h:64 * h + 64, b, :], cst[32 * par:32 * par + 1, C_ONE:C_ONE + CW],
                                  brow[32 * par:32 * par + 1, m * D + h * 512:m * D + (h + 1) * 512],
                                  start=True, stop=False, tile_position=(32 * par, 64 * h))
                for r in range(first_r, first_r + 4):
                    s = phys((c * EP + r) % RING)
                    pe.wait_ge(slot_full[s], uses(s, c * EP + r))
                    w = ring[:, s, :].rearrange("p (k n) -> p k n", k=2)
                    for k2 in range(2):
                        k = 2 * (r % 4) + k2
                        for h in range(2):
                            mm = pe.matmul(psum[64 * h:64 * h + 64, b, :], src[:, k, :], w[:, k2, h * 512:(h + 1) * 512],
                                           start=(bias is None and k == 0), stop=(k == KB - 1),
                                           tile_position=(0, 64 * h))
                    mm.then_inc(weights_used, 1)

            def scatter(nth, chunk):
                pe.wait_ge(ysb_ready, chunk + 1)
                pe.wait_ge(S_ready, chunk + 1)
                for t in range(TT):
                    for h in range(2):
                        mm = pe.matmul(bank(2 * t + h), S[64 * h:64 * h + 64, t * P:(t + 1) * P],
                                       ysb[64 * h:64 * h + 64, :], start=False, stop=False, skip_group_check=True,
                                       tile_position=(64 * h, 0))
                mm.then_inc(scattered, 1)

            def turn_weights(j):
                pe.wait_ge(Gw_ready, j + 1)
                for t in range(TT):
                    tr = pe.transpose(bank(4, t * P, P), Gw[:, t, :, :].rearrange("p h c -> p (h c)"), ident)
                tr.then_inc(S_turned, 1)

            def turn_act(j):
                pe.wait_ge(act_ready, j + 1)
                for b in range(4):
                    tr = pe.transpose(bank(5, b * P, P), act[:, b * P:(b + 1) * P], ident)
                tr.then_inc(act_turned, 1)

            pe.wait_ge(part_ready, 3)
            pe.wait_ge(h2T_ready, 4)
            gather(0)
            pe.wait_ge(wgt_ready, 1)
            for t in range(TT):
                tr = pe.transpose(psum[0:NE, 5, t * P:(t + 1) * P], wgt[:, t, 0:NE], ident)
            tr.then_inc(wT_turned, 1)
            pe.wait_ge(wT_ready, 1)
            pe.wait_ge(bdn_in, 16)
            pe.wait_ge(x1_ready, NKV)
            for t in range(TT):
                for h in range(2):
                    pe.matmul(bank(2 * t + h), wT[:, t * P:(t + 1) * P], bdn[:, h * 512:(h + 1) * 512], start=True,
                              stop=False, skip_group_check=True)
            with pe.Fori(0, NE // UNROLL) as it:
                def uses(s, p):
                    return it * (16 * UNROLL * EP // RING) + 16 * (uses1(s) + p // RING + 1)
                for c in range(UNROLL):
                    j = it * UNROLL + c
                    pe.wait_ge(bias_full[c % 2], it * (32 * UNROLL // 2) + 32 * (c // 2 + 1))
                    pe.wait_ge(xe_ready, j + 1)
                    pe.wait_ge(S_ready, j + 1)
                    wide(4, xe, c, 0, uses, (c % 2, 0))
                    wide(5, xe, c, 4, uses, (c % 2, 1))
                    scatter(j, j)
                    gather(j + 1)
                    turn_act(j)
                    turn_weights(j)
                    pe.wait_ge(aT_ready, j + 1)
                    wide(7, aT, c, 8, uses, None)
            scatter(NE, NE)

            pe.wait_ge(nov_ready, 1)
            nov = pe.value_load(novt[0:1, 0:1], min_val=0, max_val=NJ)
            with pe.If(nov > 0):
                for t in range(TT):
                    pe.transpose(psum[0:NE, 6, t * P:(t + 1) * P], pos[:, t, 0:NE], ident)
                for t in range(TT):
                    mm = pe.matmul(psum[0:NE, 6, 256:257], Mf[:, t, :], cst[:, C_ONE:C_ONE + 1], start=(t == 0),
                                   stop=(t == TT - 1))
                mm.then_inc(ov_pe, 1)
                pe.wait_ge(ov_dve, 1)
                pe.matmul(psum[0:NE, 6, 300:301], tri[0:NE, 0:NE], ovn, start=True, stop=True).then_inc(ov_pe, 1)
                pe.wait_ge(ov_dve, 2)
                pe.matmul(psum[0:1, 6, 320:320 + NJ], cst[0:NE, C_COL:C_COL + 1], ovE, start=True, stop=True)
                for t in range(TT):
                    pe.matmul(bank(6, 352 + t * NJ, NJ), wT[:, t * P:(t + 1) * P], ovE, start=True, stop=True)
                for t in range(TT):
                    pe.matmul(bank(6, 352 + (2 + t) * NJ, NJ), posT[:, t * P:(t + 1) * P], ovE, start=True, stop=False)
                    mm = pe.matmul(bank(6, 352 + (2 + t) * NJ, NJ), ones[0:NE, :], ovK, start=False, stop=True)
                mm.then_inc(ov_pe, 1)
                with pe.Fori(0, nov) as j:
                    def uses(s, p):
                        return j * 16 + 16 * (uses1(s) + NE * EP // RING + 1)
                    gather(j + (NE + 1))
                    pe.wait_ge(bias_full[0], j * 32 + 32 * (NE // 2 + 1))
                    pe.wait_ge(xe_ready, j + (NE + 2))
                    wide(4, xe, 0, 0, uses, (0, 0))
                    wide(5, xe, 0, 4, uses, (0, 1))
                    turn_act(j + NE)
                    turn_weights(j + NE)
                    pe.wait_ge(aT_ready, j + (NE + 1))
                    wide(7, aT, 0, 8, uses, None)
                    scatter(j + (NE + 1), j + (NE + 1))

        @block.scalar
        def _(act_e):
            act_e.dma_start(cst[:, :], A["constants"]).then_inc(cst_in, 16)
            act_e.dma_start(params[0:8, :], A["g_mix"][0].rearrange("(r c) -> r c", c=P)).then_inc(par_in, 16)
            act_e.dma_start(params[8:60, :], A["b_in"][0].rearrange("(r c) -> r c", c=P)).then_inc(par_in, 16)
            act_e.dma_start(params[60:84, :], A["w_conv"][0].rearrange("j (r c) -> (j r) c", c=P)).then_inc(par_in, 16)
            act_e.dma_start(bv, A["b_in"][0:1, VCOL * PW:(VCOL + 1) * PW].partition_broadcast(P)).then_inc(small_in, 16)
            act_e.dma_start(snk[:, :], A["sinks"][0:1, :].partition_broadcast(P)).then_inc(small_in, 16)
            act_e.dma_start(gbc[:, :], A["g_ffn"][0:1, :].partition_broadcast(P)).then_inc(small_in, 16)
            act_e.dma_start(wr[:, :, :], A["w_router"][0].rearrange("(k p) e -> p k e", p=P)).then_inc(small_in, 16)
            act_e.dma_start(brt[:, :], A["b_router"][0:1, :].partition_broadcast(P)).then_inc(small_in, 16)

            def square_sums(col):
                for t in range(TT):
                    nc.scalar.activation(normed[:, t, :], xres[:, t, :], ACT.Square,
                                         accum_out=small[:, col + t:col + t + 1]).then_inc(ssq_ready, 1)

            act_e.wait_ge(x_in, 16)
            square_sums(0)
            act_e.wait_ge(par_ready, 1)
            act_e.wait_ge(piece_done, 1)
            for b in range(2):
                ins = nc.scalar.activation(raw[:, b, :], psum[:, 7, b * T:(b + 1) * T], ACT.Identity,
                                           bias=bT[:, 2 * KCOL + b:2 * KCOL + b + 1])
            ins.then_inc(raw_ready, 1)

            act_e.wait_ge(kz_ready, 1)
            act_e.wait_ge(rotated, 1)
            for kv in range(NKV):
                a = 64 * (kv % 2)
                for h in range(2):
                    nc.scalar.copy(kz[64 * h:64 * h + 64, kv, h, :], kT[a:a + 64, kv // 2, :]).then_inc(kz_ready, 1)

            with act_e.Fori(0, NKV) as i:
                act_e.wait_ge(piece_done, i * 6 + 3)
                act_e.wait_ge(rotated, i + 1)
                for b in range(2):
                    ins = nc.scalar.activation(raw[:, b, :], psum[:, 2, b * T:(b + 1) * T], ACT.Identity,
                                               bias=bT[:, bass.ds(i * 2 + b, 1)])
                ins.then_inc(raw_ready, 1)
                act_e.wait_ge(piece_done, i * 6 + 4)
                for b in range(2):
                    ins = nc.scalar.activation(ccs[:, b, :], psum[:, 0, b * T:(b + 1) * T], ACT.Identity,
                                               bias=bT[:, bass.ds(i * 2 + (2 * CC + b), 1)])
                ins.then_inc(cc_ready, 1)
                act_e.wait_ge(max_ready, i + 1)
                nc.scalar.activation(small[:, 32:40], small[:, 32:40], ACT.Exp)
                for t in range(TT):
                    for h in range(4):
                        n, at = t * 4 + h, (h * P, 512 + h * T)[t]
                        s = sm[:, at:at + (t + 1) * P]
                        ins = nc.scalar.activation(s, s, ACT.Exp, bias=small[:, 16 + n:17 + n],
                                                   accum_out=small[:, 24 + n:25 + n])
                ins.then_inc(exp_ready, 1)
                for which, b, col, due in ((ga, 0, GA, 7), (gc, 1, GC, 8)):
                    act_e.wait_ge(piece_done, i * 6 + due)
                    for m in range(2):
                        ins = nc.scalar.activation(which[:, bass.ds(i * 2 + m, 1), :].rearrange("p a t -> p (a t)"),
                                                   psum[:, b, m * T:(m + 1) * T], ACT.Sigmoid,
                                                   bias=bT[:, bass.ds(i * 2 + (2 * col + m), 1)])
                    ins.then_inc(gates_ready, 1)
                    if which is ga:
                        act_e.wait_ge(pT_turned, i + 1)
                        nc.scalar.copy(pT[:, 0:4, :].rearrange("p n q -> p (n q)"), psum[:, 3, :]).then_inc(pT_ready, 1)
                        nc.scalar.copy(pT[:, 4:12, :].rearrange("p n q -> p (n q)"),
                                       psum[:, 4:6, :].rearrange("p b n -> p (b n)")).then_inc(pT_ready, 1)
                act_e.wait_ge(o_ready, i + 1)
                nc.scalar.copy(attnT[:, bass.ds(i * 2, 2), :].rearrange("p m t -> p (m t)"),
                               psum[:, 6, :]).then_inc(bank6_read, 1)
                act_e.wait_ge(u_ready, i + 1)

            act_e.wait_ge(merged_ready, NKV)
            act_e.dma_start(bdn, A["b_down"][0]).then_inc(bdn_in, 16)
            act_e.wait_ge(x1_ready, NKV)
            square_sums(6)
            act_e.wait_ge(normed_ready, 4)
            for b in range(4):
                act_e.wait_ge(h2T_turned, b + 1)
                nc.scalar.copy(mt[:, 2 * b:2 * b + 2, :].rearrange("p k t -> p (k t)"), psum[:, 3 + b, :]).then_inc(h2T_ready, 1)
            nc.scalar.copy(h2b[:, 0, :, :], normed[:, :, :]).then_inc(part_ready, 1)
            act_e.dma_start(gbc[:, :], A["g_final"].rearrange("(a d) -> a d", a=1).partition_broadcast(P)).then_inc(gfin_in, 16)
            act_e.wait_ge(shifted_ready, 1)
            nc.scalar.activation(topw, topw, ACT.Exp).then_inc(topexp_ready, 1)
            act_e.wait_ge(rest_ready, 1)
            nc.scalar.copy(h2b[:, 1, :, :], normed[:, :, :]).then_inc(part_ready, 1)

            def take_gathered(nth):
                act_e.wait_ge(gathered, nth + 1)
                nc.scalar.copy(xe.rearrange("p k c -> p (k c)"), psum[:, 6, :]).then_inc(xe_ready, 1)

            def take_act(j):
                act_e.wait_ge(act_turned, j + 1)
                nc.scalar.copy(aT.rearrange("p (h b) c -> p b h c", h=2),
                               psum[:, 5, :].rearrange("p (b h c) -> p b h c", b=4, h=2)).then_inc(aT_ready, 1)

            def take_y(used):
                act_e.wait_ge(weights_used, used)
                nc.scalar.copy(ysb, psum[:, 7, :]).then_inc(ysb_ready, 1)

            def squash(j):
                act_e.wait_ge(gmin_ready, j + 1)
                nc.scalar.activation(sg, gm, ACT.Sigmoid, scale=ALPHA).then_inc(sig_ready, 1)

            act_e.wait_ge(ysb_ready, 1)
            take_gathered(0)
            act_e.wait_ge(wT_turned, 1)
            nc.scalar.copy(wT[:, :], psum[0:NE, 5, 0:256]).then_inc(wT_ready, 1)
            with act_e.Fori(0, NE // UNROLL) as it:
                for c in range(UNROLL):
                    j = it * UNROLL + c
                    squash(j)
                    take_gathered(j + 1)
                    take_act(j)
                    take_y(it * (UNROLL * EP) + (c + 1) * EP)
            act_e.wait_ge(nov_ready, 1)
            nov = act_e.value_load(novt[0:1, 0:1], min_val=0, max_val=NJ)
            with act_e.If(nov > 0):
                with act_e.Fori(0, nov) as j:
                    take_gathered(j + (NE + 1))
                    squash(j + NE)
                    take_act(j + NE)
                    take_y(j * EP + (NE + 1) * EP)
            act_e.wait_ge(x2_ready, 1)
            square_sums(48)

        @block.vector
        def _(dve):
            v = nc.vector
            steps = Steps(dve, dve_step)

            def ms(col):
                v.tensor_scalar(small[:, col + 2:col + 4], small[:, col:col + 2], 1.0 / D, EPS, ALU.mult,
                                ALU.add).then_inc(ms_ready, 1)

            def rotate(dst):
                for quarter in range(4):
                    a, b = 32 * quarter, 32 * (quarter ^ 1)
                    ins = v.tensor_copy(swp[a:a + 32, :, :], raw[b:b + 32, :, :])
                steps.link(ins)
                cos = cst[:, C_COS:C_COS + T].unsqueeze(1).broadcast_to([P, 2, T])
                sin = cst[:, C_SIN:C_SIN + T].unsqueeze(1).broadcast_to([P, 2, T])
                v.tensor_tensor(dst, raw, cos, ALU.mult)
                steps.link(v.tensor_tensor(swp, swp, sin, ALU.mult))
                v.tensor_tensor(dst, dst, swp, ALU.add).then_inc(rotated, 1)

            dve.wait_ge(cst_in, 16)
            v.memset(u[:, :, 0:2], 0.0)
            v.memset(pos[:, :, NE:NE + 1], NEVER)
            v.memset(wgt[:, :, NE:NE + 1], 0.0)
            steps.link(v.tensor_copy(tri16[:, :], cst[:, C_TRI:C_TRI + 2 * P]))
            dve.wait_ge(ssq_ready, 2)
            ms(0)
            dve.wait_ge(rstd_ready, 1)
            for t in range(TT):
                v.tensor_scalar(normed[:, t, :], xres[:, t, :], small[:, 4 + t:5 + t], None, ALU.mult).then_inc(normed_ready, 1)
            dve.wait_ge(par_turned, 1)
            v.tensor_copy(parT[:, :], psum[:, 7, 0:84]).then_inc(par_ready, 1)
            dve.wait_ge(par_ready, 1)
            for k in range(KB):
                dve.wait_ge(x_turned, k // 2 + 1)
                v.tensor_scalar(hT[:, k, :], psum[:, 3 + k // 2, (k % 2) * T:(k % 2 + 1) * T], g1T[:, k:k + 1], None,
                                ALU.mult).then_inc(hT_ready, 1)
            dve.wait_ge(raw_ready, 1)
            rotate(kT)
            dve.wait_ge(piece_done, 2)
            dve.wait_ge(small_in, 16 * 5)
            v.tensor_tensor(V, psum[:, 6, :].rearrange("p (t c) -> p t c", t=TT), bv.unsqueeze(1).broadcast_to([P, TT, PW]),
                            ALU.add).then_inc(bank6_read, 1)

            with dve.Fori(0, NKV) as i:
                steps.begin_loop(i, 10)
                dve.wait_ge(raw_ready, i + 2)
                rotate(q)
                dve.wait_ge(scores_ready, i + 1)
                s0 = sm[:, 0:512].rearrange("p (h s) -> p h s", h=4)
                s1 = sm[:, 512:1536].rearrange("p (h s) -> p h s", h=4)
                v.scalar_tensor_tensor(s0, psum[:, 3, :].rearrange("p (h s) -> p h s", h=4), HD ** -0.5,
                                       cst[:, C_M0:C_M0 + P].unsqueeze(1).broadcast_to([P, 4, P]), ALU.mult, ALU.add)
                steps.link(v.scalar_tensor_tensor(
                    s1, psum[:, 4:6, :].rearrange("p b (h s) -> p (b h) s", h=2), HD ** -0.5,
                    cst[:, C_M1:C_M1 + T].unsqueeze(1).broadcast_to([P, 4, T]), ALU.mult, ALU.add))
                v.tensor_reduce(small[:, 8:12], s0, AX.X, ALU.max)
                steps.link(v.tensor_reduce(small[:, 12:16], s1, AX.X, ALU.max))
                mx = small[:, 8:16].rearrange("p (t h) -> p t h", t=TT)
                sink = snk[:, bass.ds(i * 4, 4)].unsqueeze(1).broadcast_to([P, TT, 4])
                steps.link(v.tensor_tensor(mx, mx, sink, ALU.max))
                v.tensor_tensor(small[:, 32:40].rearrange("p (t h) -> p t h", t=TT), sink, mx, ALU.subtract)
                v.tensor_scalar(small[:, 16:24], small[:, 8:16], -1.0, None, ALU.mult).then_inc(max_ready, 1)
                dve.wait_ge(piece_done, i * 6 + 5)
                dve.wait_ge(cc_ready, i + 1)
                for b in range(2):
                    ins = v.scalar_tensor_tensor(u[:, b, 2:T + 2], psum[:, 1, b * T:(b + 1) * T],
                                                 bT[:, bass.ds(i * 2 + (2 * CX + b), 1)], ccs[:, b, :], ALU.add, ALU.mult)
                ins.then_inc(u_ready, 1)
                dve.wait_ge(u_ready, i + 1)
                for tap in range(3):
                    for b in range(2):
                        w = wcT[:, bass.ds(i * 2 + (8 * tap + b), 1)]
                        if tap == 0:
                            ins = v.tensor_scalar(ycv[:, b, :], u[:, b, 0:T], w, None, ALU.mult)
                        else:
                            ins = v.scalar_tensor_tensor(ycv[:, b, :], u[:, b, tap:tap + T], w, ycv[:, b, :], ALU.mult, ALU.add)
                    steps.link(ins)
                dve.wait_ge(exp_ready, i + 1)
                steps.link(v.tensor_tensor(small[:, 24:32], small[:, 24:32], small[:, 32:40], ALU.add))
                steps.link(v.reciprocal(small[:, 40:48], small[:, 24:32]))
                v.tensor_tensor(s0, s0, small[:, 40:44].unsqueeze(2).broadcast_to([P, 4, P]), ALU.mult)
                v.tensor_tensor(s1, s1, small[:, 44:48].unsqueeze(2).broadcast_to([P, 4, T]), ALU.mult).then_inc(p_ready, 1)
                dve.wait_ge(piece_done, i * 6 + 6)
                for b in range(2):
                    ins = v.scalar_tensor_tensor(zT[:, bass.ds(i * 2 + b, 1), :].rearrange("p a t -> p (a t)"),
                                                 psum[:, 2, b * T:(b + 1) * T], bT[:, bass.ds(i * 2 + (2 * CB + b), 1)],
                                                 ycv[:, b, :], ALU.add, ALU.mult)
                ins.then_inc(z_ready, 1)
                dve.wait_ge(pT_turned, i + 1)
                steps.end_loop(NKV)

            dve.wait_ge(gates_ready, 2 * NKV)
            n = NIN
            flat = lambda x: x.rearrange("p m t -> p (m t)")
            for i in range(NKV):
                if i:
                    dve.wait_ge(merged_ready, i)
                for gate, tmp in ((gc, raw), (ga, swp)):
                    dve.wait_ge(piece_done, n + 1)
                    v.tensor_tensor(flat(tmp), psum[:, n % 3, :], flat(gate[:, 2 * i:2 * i + 2, :]), ALU.mult).then_inc(branch_read, 1)
                    n += 1
                dve.wait_ge(branch_read, 2 * (i + 1))
                v.tensor_tensor(mt[:, 2 * i:2 * i + 2, :], raw, swp, ALU.add).then_inc(merged_ready, 1)
            dve.wait_ge(merged_ready, NKV)
            v.memset(S, 0.0).then_inc(S_ready, 1)
            v.memset(ysb, 0.0).then_inc(ysb_ready, 1)
            for i in range(NKV):
                dve.wait_ge(piece_done, n + 1)
                xs = xres[:, :, i * PW:(i + 1) * PW]
                v.tensor_tensor(xs, psum[:, n % 3, :].rearrange("p (t c) -> p t c", t=TT), xs, ALU.add).then_inc(x1_ready, 1)
                n += 1
            dve.wait_ge(ssq_ready, 4)
            ms(6)
            dve.wait_ge(rstd_ready, 2)
            for t in range(TT):
                v.scalar_tensor_tensor(normed[:, t, :], xres[:, t, :], small[:, 10 + t:11 + t], gbc[:, :], ALU.mult,
                                       ALU.mult).then_inc(normed_ready, 1)

            dve.wait_ge(logits_ready, 1)
            steps.link(v.tensor_tensor(lg, psum[:, 7, 0:2 * NE].rearrange("p (t e) -> p t e", t=TT),
                                       brt[:, :].unsqueeze(1).broadcast_to([P, TT, NE]), ALU.add))
            for t in range(TT):
                ins = v.max(top8[:, t, :], lg[:, t, :])
            steps.link(ins)
            v.tensor_tensor(topw, top8[:, :, 0:TOPK], top8[:, :, 0:1].broadcast_to([P, TT, TOPK]),
                            ALU.subtract).then_inc(shifted_ready, 1)
            for t in range(TT):
                ins = v.max_index(topi[:, t, :], top8[:, t, :], lg[:, t, :])
            steps.link(ins)
            steps.link(v.tensor_copy(topf, topi[:, :, :]))
            for t in range(TT):
                ins = v.tensor_tensor(onehot[:, t], count_up[:, 0:NE].unsqueeze(1).broadcast_to([P, TOPK, NE]),
                                      topf[:, t, 0:TOPK].unsqueeze(2).broadcast_to([P, TOPK, NE]), ALU.is_equal)
            steps.link(ins)
            for t in range(TT):
                ins = v.tensor_reduce(Mf[:, t, :], onehot[:, t].rearrange("p k e -> p e k"), AX.X, ALU.add)
            steps.link(ins)
            v.tensor_copy(Mb[:, :, :], Mf[:, :, :]).then_inc(M_ready, 1)
            dve.wait_ge(topexp_ready, 1)
            steps.link(v.tensor_reduce(tops, topw, AX.X, ALU.add))
            steps.link(v.reciprocal(tops, tops))
            steps.link(v.tensor_tensor(topw, topw, tops.unsqueeze(2).broadcast_to([P, TT, TOPK]), ALU.mult))
            for t in range(TT):
                ins = v.tensor_tensor(onehot[:, t], onehot[:, t], topw[:, t, :].unsqueeze(2).broadcast_to([P, TOPK, NE]),
                                      ALU.mult)
            steps.link(ins)
            for t in range(TT):
                ins = v.tensor_reduce(wgt[:, t, 0:NE], onehot[:, t].rearrange("p k e -> p e k"), AX.X, ALU.add)
            ins.then_inc(wgt_ready, 1)
            dve.wait_ge(ranks_ready, 1)
            steps.link(v.scalar_tensor_tensor(pos[:, :, 0:NE], psum[:, 7, 64:128].rearrange("p (t e) -> p t e", t=TT),
                                              -NEVER, Mf[:, :, :], ALU.add, ALU.mult))
            steps.link(v.tensor_scalar(pos[:, :, 0:NE], pos[:, :, 0:NE], NEVER, None, ALU.add))

            def one_hot(nth, table, at):
                if not isinstance(nth, int):
                    dve.wait_ge(gathered, nth)
                for t in range(TT):
                    ins = v.tensor_scalar(G[:, t, :], iota, table[:, t, at], None, ALU.is_equal)
                ins.then_inc(G_ready, 1)

            def one_hot_weights(j, table, weights, at):
                for t in range(TT):
                    ins = v.tensor_scalar(Gw[:, t, :, :], iota.unsqueeze(1).broadcast_to([P, 2, CW]), table[:, t, at],
                                          weights[:, t, at], ALU.is_equal, ALU.mult)
                ins.then_inc(Gw_ready, 1)

            def swiglu(j, used):
                dve.wait_ge(weights_used, used + 4)
                v.tensor_scalar(uc, psum[:, 4, :], LIMIT, -LIMIT, ALU.min, ALU.max)
                dve.wait_ge(weights_used, used + 8)
                v.tensor_scalar(gm, psum[:, 5, :], LIMIT, None, ALU.min).then_inc(gmin_ready, 1)
                dve.wait_ge(gmin_ready, j + 1)
                v.scalar_tensor_tensor(uc, uc, 1.0, gm, ALU.add, ALU.mult)
                dve.wait_ge(sig_ready, j + 1)
                steps.link(v.tensor_copy(small[:, 60:61], small[:, 0:1]))
                v.tensor_tensor(act, uc, sg, ALU.mult).then_inc(act_ready, 1)

            def take_weights(j):
                dve.wait_ge(S_turned, j + 1)
                v.tensor_copy(S, psum[:, 4, 0:256]).then_inc(S_ready, 1)

            one_hot(0, pos, slice(0, 1))
            steps.link(v.tensor_copy(cnt[:, :], psum[:, 7, 128:128 + NE]))
            for k in range(NK):
                ins = v.tensor_scalar(more[:, k * NE:(k + 1) * NE], cnt[:, :], float((k + 1) * CAP), None, ALU.is_gt)
            steps.link(ins)
            steps.link(v.tensor_reduce(small[:, 54:55], more[:, :], AX.X, ALU.add))
            v.tensor_copy(novt[:, :], small[:, 54:55]).then_inc(nov_ready, 1)

            with dve.Fori(0, NE // UNROLL) as it:
                steps.begin_loop(it, UNROLL)
                for c in range(UNROLL):
                    j = it * UNROLL + c
                    one_hot_weights(j, pos, wgt, bass.ds(j, 1))
                    one_hot(j + 1, pos, bass.ds(j + 1, 1))
                    swiglu(j, it * (UNROLL * EP) + c * EP)
                    take_weights(j)
                steps.end_loop(NE // UNROLL)

            nov = dve.value_load(novt[0:1, 0:1], min_val=0, max_val=NJ)
            with dve.If(nov > 0):
                dve.wait_ge(ov_pe, 1)
                v.tensor_copy(posT, psum[0:NE, 6, 0:T])
                for k in range(NK):
                    ins = v.tensor_scalar(ovF[:, k:k + 1], psum[0:NE, 6, 256:257], float((k + 1) * CAP), None, ALU.is_gt)
                steps.link(ins)
                v.tensor_reduce(ovn, ovF, AX.X, ALU.add).then_inc(ov_dve, 1)
                dve.wait_ge(ov_pe, 2)
                v.tensor_copy(ovo, psum[0:NE, 6, 300:301])
                v.memset(ovE, 0.0)
                steps.link(v.memset(ovK, 0.0))
                for k in range(NK):
                    steps.link(v.tensor_scalar(ovR, count_up[0:NE, 0:NJ], ovo, float(k), ALU.subtract, ALU.is_equal))
                    steps.link(v.tensor_scalar(ovR, ovR, ovF[:, k:k + 1], None, ALU.mult))
                    v.tensor_tensor(ovE, ovE, ovR, ALU.add)
                    steps.link(v.scalar_tensor_tensor(ovK, ovR, float(-CAP * (k + 1)), ovK, ALU.mult, ALU.add))
                v.tensor_copy(small[:, 61:62], small[:, 0:1]).then_inc(ov_dve, 1)
                dve.wait_ge(ov_pe, 3)
                v.tensor_copy(wgtO, psum[:, 6, 352:352 + 2 * NJ].rearrange("p (t j) -> p t j", t=TT))
                v.tensor_copy(posO, psum[:, 6, 352 + 2 * NJ:352 + 4 * NJ].rearrange("p (t j) -> p t j", t=TT))
                v.tensor_copy(eid[:, :], psum[0:1, 6, 320:320 + NJ]).then_inc(ov_dve, 1)
                dve.wait_ge(ov_dve, 3)
                at0 = steps.n
                with dve.Fori(0, nov) as j:
                    steps.begin_loop(j, 1)
                    one_hot(j + (NE + 1), posO, bass.ds(j, 1))
                    one_hot_weights(j + NE, posO, wgtO, bass.ds(j, 1))
                    swiglu(j + NE, j * EP + NE * EP)
                    take_weights(j + NE)
                    steps.base = steps.before
            dve.wait_ge(scattered, nov + (NE + 1))
            for t in range(TT):
                ins = v.tensor_tensor(xres[:, t, :], psum[:, 2 * t:2 * t + 2, :].rearrange("p h n -> p (h n)"), xres[:, t, :], ALU.add)
            ins.then_inc(x2_ready, 1)
            dve.wait_ge(ssq_ready, 6)
            ms(48)
            dve.wait_ge(rstd_ready, 3)
            dve.wait_ge(gfin_in, 16)
            for t in range(TT):
                v.scalar_tensor_tensor(normed[:, t, :], xres[:, t, :], small[:, 52 + t:53 + t], gbc[:, :], ALU.mult,
                                       ALU.mult).then_inc(out_ready, 1)

        @block.gpsimd
        def _(pool):
            g = nc.gpsimd

            def rstd(nth, col):
                pool.wait_ge(ms_ready, nth)
                g.tensor_tensor(small[:, col + 4:col + 6], small[:, col + 2:col + 4],
                                cst[:, C_COL + 1:C_COL + 2].broadcast_to([P, 2]), ALU.pow).then_inc(rstd_ready, 1)

            g.memset(kz, 0.0).then_inc(kz_ready, 1)
            pool.wait_ge(cst_in, 16)
            rstd(1, 0)
            pool.wait_ge(bank6_read, 1)
            with pool.Fori(0, NKV) as i:
                g.tensor_copy(vcur, V[:, :, bass.ds(i * HD, HD)]).then_inc(vcur_ready, 1)
                pool.wait_ge(o_ready, i + 1)
            rstd(2, 6)
            pool.wait_ge(part_ready, 1)
            pool.wait_ge(h2T_turned, 4)
            g.tensor_tensor(normed[:, :, :], normed[:, :, :], h2b[:, 0, :, :], ALU.subtract).then_inc(rest_ready, 1)
            pool.wait_ge(part_ready, 2)
            pool.wait_ge(rest_ready, 1)
            g.tensor_tensor(h2b[:, 2, :, :], normed[:, :, :], h2b[:, 1, :, :], ALU.subtract).then_inc(part_ready, 1)
            rstd(3, 48)


_INS = ["x", "g_mix", "w_in", "b_in", "sinks", "w_conv", "w_attn_o", "w_conv_o", "w_out", "g_ffn", "w_router", "b_router",
        "w_gate", "b_gate", "w_up", "b_up", "w_down", "b_down", "g_final"]


def kernel(**inputs):
    import concourse.bacc as _bacc
    from concourse.bass_utils import run_bass_kernel_spmd as _run

    nc = _bacc.Bacc("TRN2", target_bir_lowering=False, num_devices=1)
    arrays, args = {}, {}
    given = {name: np.ascontiguousarray(inputs[name]) for name in _INS}
    given["constants"] = shape_constants()
    for name, a in given.items():
        arrays[f"in_{name}"] = a
        args[name] = nc.dram_tensor(f"in_{name}", a.shape, mybir.dt.from_np(a.dtype), kind="ExternalInput").ap()
    out = nc.dram_tensor("out_0", (1, T, D), F32, kind="ExternalOutput").ap()
    hybrid_block(nc, args, out)
    r = _run(nc, [arrays], core_ids=[0])
    return r.results[0]["out_0"]
```

```python
from contextlib import ExitStack

import concourse.bass as bass
import numpy as np
from concourse import mybir

F32 = mybir.dt.float32
F32R = mybir.dt.float32r
BF16 = mybir.dt.bfloat16
I32 = mybir.dt.int32
U32 = mybir.dt.uint32
ALU = mybir.AluOpType
ACT = mybir.ActivationFunctionType
AX = mybir.AxisListType

P = 128
D = 1024
KB = D // P
T = 256
TT = T // P
HD = 64
NQ = D // HD
NKV = NQ // 4
NE = 32
TOPK = 4
EPS = 1e-5
LIMIT, ALPHA = 7.0, 1.702
CW = 64
CAP = 64
NJ = T * TOPK // CAP - 1
NK = T // CAP - 1
NEVER = 999.0
MASKED = -3.0e38

PW = 256
NIN = 6 * NKV + 2
NP1 = NIN + 12
RING1 = 3
RING = 16
PHYS = [3, 4, 11, 9, 10, 5, 6, 7, 8, 0, 1, 2, 12, 13, 14, 15]
EP = 12
UNROLL = 4
assert EP * UNROLL % RING == 0 and NE % UNROLL == 0

C_ID, C_TRI, C_ONE, C_M0, C_M1 = 0, 128, 256, 384, 512
C_IOTA = 768
C_COS, C_SIN = 832, 1088
C_COL = 1344
C_UP = 1346
C_W = 1410


def shape_constants():
    c = np.zeros((P, C_W), np.float32)
    p = np.arange(P)
    c[:, C_ID:C_ID + P] = np.eye(P)
    c[:, C_TRI:C_TRI + P] = p[:, None] < p[None, :]
    c[:, C_ONE:C_ONE + P] = 1.0
    c[:, C_M0:C_M0 + P] = np.where(p[None, :] <= p[:, None], 0.0, MASKED)
    dist = p[:, None] + P - np.arange(2 * P)[None, :]
    c[:, C_M1:C_M1 + 2 * P] = np.where((dist >= 0) & (dist < P), 0.0, MASKED)
    c[:, C_IOTA:C_IOTA + CW] = np.where(np.arange(CW) < CAP, np.arange(CW), -5 * T)
    half = HD // 2
    inv = np.float32(10000.0) ** (-np.arange(half, dtype=np.float32) / np.float32(half))
    ang = np.arange(T, dtype=np.float32)[None, :] * inv[p % half][:, None]
    c[:, C_COS:C_COS + T] = np.cos(ang)
    c[:, C_SIN:C_SIN + T] = np.sin(ang) * np.where(p % HD < half, -1.0, 1.0)[:, None]
    c[:, C_COL] = p
    c[:, C_UP:C_UP + CW] = np.arange(CW)
    c[:, C_COL + 1] = -0.5
    return c


class Steps:

    def __init__(self, eng, sem):
        self.eng, self.sem, self.n, self.base = eng, sem, 0, 0

    def link(self, ins):
        ins.then_inc(self.sem, 1)
        self.n += 1
        self.eng.wait_ge(self.sem, self.base + self.n)

    def begin_loop(self, i, per_turn):
        self.at, self.per_turn, self.before = self.n, per_turn, self.base
        self.base = self.before + i * per_turn

    def end_loop(self, turns):
        assert self.n - self.at == self.per_turn, (self.n - self.at, self.per_turn)
        self.base = self.before
        self.n = self.at + self.per_turn * turns


def hybrid_block(nc, A, out):
    ctx = ExitStack()
    with ctx:
        def sb(name, shape, dt=F32):
            return ctx.enter_context(nc.sbuf_tensor(name, shape, dt))

        def sem(name):
            return ctx.enter_context(nc.semaphore(name))

        ring_at = -(-nc.sbuf_base // 32) * 32
        ring = sb("ring", [P, RING, KB * PW])
        cst = sb("cst", [P, C_W])
        xres = sb("xres", [P, TT, D])
        normed_at = -(-nc.sbuf_base // 32) * 32
        normed = sb("normed", [P, TT, D])
        ph1_at = -(-nc.sbuf_base // 32) * 32
        h2b = sb("h2b", [P, 3, TT, D], BF16)
        mt_at = -(-nc.sbuf_base // 32) * 32
        mt = sb("mt", [P, KB, T])
        gbc = sb("gbc", [P, D])
        wr = sb("wr", [P, KB, NE])
        brow = sb("brow", [33, 2 * D])
        work = sb("work", [P, 5120])
        params = sb("params", [84, P])
        parT = sb("parT", [P, 84])
        snk = sb("snk", [P, NQ])
        brt = sb("brt", [P, NE])
        small = sb("small", [P, 64])
        G = sb("G", [P, TT, CW], BF16)
        tri16 = sb("tri16", [P, 2 * P], BF16)
        pos = sb("pos", [P, TT, NE + 1])
        wgt = sb("wgt", [P, TT, NE + 1])
        Mf = sb("Mf", [P, TT, NE])
        Mb = sb("Mb", [P, TT, NE], BF16)
        cnt = sb("cnt", [P, NE])
        novt = sb("novt", [P, 1], I32)
        psum = ctx.enter_context(nc.psum_tensor("psum", [P, 8, 512], F32))

        def slot(s):
            return ring[:, s, :]
        def parts(name, at, shape):
            return nc.alloc_sbuf_tensor_at(name, shape, F32R, offset=at)

        def at_slot(s):
            return ring_at + s * KB * PW * 4
        hH, hL = parts("hH", at_slot(3), [P, KB, T]), parts("hL", at_slot(4), [P, KB, T])
        zH, zL = parts("zH", at_slot(5), [P, KB, T]), parts("zL", at_slot(6), [P, KB, T])
        aH, aL = parts("aH", at_slot(7), [P, KB, T]), parts("aL", at_slot(8), [P, KB, T])
        wH, wL = (parts("wH", at_slot(12), [P, 2, 2, KB, P]),
                  parts("wL", at_slot(14), [P, 2, 2, KB, P]))
        mH, mL = parts("mH", mt_at, [P, KB, T]), parts("mL", normed_at, [P, KB, T])
        ga = slot(9).rearrange("p (k t) -> p k t", k=KB)
        gc = slot(10).rearrange("p (k t) -> p k t", k=KB)
        kz = slot(11).rearrange("p (g h t) -> p g h t", g=NKV, h=2)
        ph1 = nc.alloc_sbuf_tensor_at("ph1", [P, 3072], F32, offset=ph1_at)
        kT = ph1[:, 0:512].rearrange("p (b t) -> p b t", b=2)
        V = ph1[:, 512:1024].rearrange("p (a c) -> p a c", a=TT)
        vcur = ph1[:, 1024:1152].rearrange("p (a c) -> p a c", a=TT)
        q = ph1[:, 1152:1664].rearrange("p (b t) -> p b t", b=2)
        sm = work[:, 0:1536]
        pT = work[:, 1536:3072].rearrange("p (n q) -> p n q", q=P)
        raw = work[:, 3072:3584].rearrange("p (b t) -> p b t", b=2)
        swp = work[:, 3584:4096].rearrange("p (b t) -> p b t", b=2)
        ccs = ph1[:, 1664:2176].rearrange("p (b t) -> p b t", b=2)
        u = work[:, 4096:4096 + 2 * (T + 2)].rearrange("p (b t) -> p b t", b=2)
        ycv = ph1[:, 2176:2688].rearrange("p (b t) -> p b t", b=2)
        Gw = work[:, 0:256].rearrange("p (t h c) -> p t h c", t=TT, h=2)
        S = work[:, 256:512]
        xe = work[:, 512:1024].rearrange("p (k c) -> p k c", k=KB)
        gm = work[:, 1024:1536]
        sg = work[:, 1536:2048]
        uc = work[:, 2048:2560]
        act = work[:, 2560:3072]
        aT = work[:, 3072:3584].rearrange("p (k c) -> p k c", k=KB)
        bdn = work[0:NE, 2560:3584]
        ysb = work[:, 3584:4096]
        onehot = work[:, 4096:4352].rearrange("p (t k e) -> p t k e", t=TT, k=TOPK)
        lg = work[:, 4352:4416].rearrange("p (t e) -> p t e", t=TT)
        top8 = work[:, 4416:4432].rearrange("p (t k) -> p t k", t=TT)
        topf = work[:, 4432:4448].rearrange("p (t k) -> p t k", t=TT)
        topw = work[:, 4448:4456].rearrange("p (t k) -> p t k", t=TT)
        tops = work[:, 4456:4458]
        topi = sb("topi", [P, TT, 8], U32)
        more = work[:, 4608:4608 + NK * NE]
        bv = ph1[:, 2688:2688 + PW]
        wT = sb("wT", [NE, T])
        posT = work[0:NE, 4096:4096 + T]
        ovF = work[0:NE, 4360:4360 + NK]
        ovn, ovo = work[0:NE, 4372:4373], work[0:NE, 4373:4374]
        ovE, ovK, ovR = (work[0:NE, 4380 + n * NJ:4380 + (n + 1) * NJ] for n in range(3))
        posO = work[:, 4608:4608 + TT * NJ].rearrange("p (t j) -> p t j", t=TT)
        wgtO = work[:, 4608 + 2 * NJ:4608 + 4 * NJ].rearrange("p (t j) -> p t j", t=TT)
        eid = sb("eid", [1, NJ], I32)

        ident, tri, ones = cst[:, C_ID:C_ID + P], cst[:, C_TRI:C_TRI + P], cst[:, C_ONE:C_ONE + P]
        iota = cst[:, C_IOTA:C_IOTA + CW]
        count_up = cst[:, C_UP:C_UP + CW]
        g1T, bT, wcT = parT[:, 0:8], parT[:, 8:60], parT[:, 60:84]

        slot_full = [sem(f"slot_full{s}") for s in range(RING)]
        weights_used = sem("weights_used")
        x_in, par_in, cst_in, small_in = sem("x_in"), sem("par_in"), sem("cst_in"), sem("small_in")
        bias_full = [sem("bias_full0"), sem("bias_full1")]
        dve_step, act_step, pool_step = sem("dve_step"), sem("act_step"), sem("pool_step")
        ssq_ready, ms_ready, rstd_ready, normed_ready = (sem("ssq_ready"), sem("ms_ready"), sem("rstd_ready"),
                                                         sem("normed_ready"))
        par_turned, par_ready, x_turned, hT_ready = sem("par_turned"), sem("par_ready"), sem("x_turned"), sem("hT_ready")
        blocks_done = sem("blocks_done")
        wH_ready = sem("wH_ready")
        wL0_ready, wL1_ready = sem("wL0_ready"), sem("wL1_ready")
        hH_ready, zH_ready, zL_ready, aH_ready = sem("hH_ready"), sem("zH_ready"), sem("zL_ready"), sem("aH_ready")
        msum_ready, mH_ready = sem("msum_ready"), sem("mH_ready")
        raw_ready, kz_ready = sem("raw_ready"), sem("kz_ready")
        rotated = sem("rotated")
        bank6_read = sem("bank6_read")
        cc_ready, u_ready, vcur_ready = sem("cc_ready"), sem("u_ready"), sem("vcur_ready")
        z_ready, gates_ready = sem("z_ready"), sem("gates_ready")
        scores_ready, max_ready, p_ready, exp_ready = (sem("scores_ready"), sem("max_ready"), sem("p_ready"),
                                                       sem("exp_ready"))
        pT_turned, pT_ready, o_ready = sem("pT_turned"), sem("pT_ready"), sem("o_ready")
        branch_read, merged_ready, x1_ready = sem("branch_read"), sem("merged_ready"), sem("x1_ready")
        h2T_turned, h2T_ready, logits_ready = sem("h2T_turned"), sem("h2T_ready"), sem("logits_ready")
        part_ready, rest_ready = sem("part_ready"), sem("rest_ready")
        shifted_ready, topexp_ready, M_ready, ranks_ready = (sem("shifted_ready"), sem("topexp_ready"),
                                                             sem("M_ready"), sem("ranks_ready"))
        nov_ready, wgt_ready, wT_turned, wT_ready = (sem("nov_ready"), sem("wgt_ready"), sem("wT_turned"),
                                                     sem("wT_ready"))
        G_ready, Gw_ready, gathered, xe_ready = sem("G_ready"), sem("Gw_ready"), sem("gathered"), sem("xe_ready")
        gmin_ready, sig_ready, act_ready = sem("gmin_ready"), sem("sig_ready"), sem("act_ready")
        act_turned, aT_ready, S_turned, S_ready, ysb_ready, scattered = (
            sem("act_turned"), sem("aT_ready"), sem("S_turned"), sem("S_ready"), sem("ysb_ready"), sem("scattered"))
        ov_pe, ov_dve = sem("ov_pe"), sem("ov_dve")
        bdn_in = sem("bdn_in")
        gfin_in, x2_ready, out_ready, out_done = sem("gfin_in"), sem("x2_ready"), sem("out_ready"), sem("out_done")

        def pieces(w):
            return w.rearrange("(k p) n -> p k n", p=P)
        w_in, w_ao, w_co, w_o = (pieces(A[n][0]) for n in ("w_in", "w_attn_o", "w_conv_o", "w_out"))
        experts = [A[n].rearrange("l e (k p) n -> (l e) p k n", p=P) for n in ("w_up", "w_gate", "w_down")]
        KCOL, VCOL = D // PW, D // PW + 1
        first = (D + 512) // PW
        CB, CC, CX, GA, GC = (first + 4 * n for n in range(5))
        body_cols = [0, CC, CX, CB, GA, GC]

        def phys(r):
            return PHYS[r]

        def uses1(s):
            return len([n for n in range(NP1) if n % RING1 == s]) if s < RING1 else 0

        block = ctx.enter_context(nc.Block())

        @block.sync
        def _(sp):
            def load1(s, src):
                sp.dma_start(ring[:, s, :].rearrange("p (k n) -> p k n", k=KB), src).then_inc(slot_full[s], 16)

            sp.dma_start(xres[:, :, :], A["x"][0].rearrange("(t p) d -> p t d", p=P)).then_inc(x_in, 16)
            load1(0, w_in[:, :, KCOL * PW:(KCOL + 1) * PW])
            load1(1, w_in[:, :, VCOL * PW:(VCOL + 1) * PW])
            load1(2, w_in[:, :, 0:PW])

            def slot_split(n):
                sp.wait_ge(wL0_ready, n + (1 - RING1))
                sp.wait_ge(wL1_ready, n + (1 - RING1))

            ahead = [(0, 1), (0, 2), (0, 3), (0, 4), (0, 5), (1, 0)]
            with sp.Fori(0, NKV - 1) as i:
                for at, (later, c) in enumerate(ahead):
                    slot_split(i * 6 + (3 + at))
                    load1((3 + at) % RING1, w_in[:, :, bass.ds(i * PW + (body_cols[c] + later) * PW, PW)])
            n = NIN - 5
            tail = [w_in[:, :, (body_cols[c] + NKV - 1) * PW:(body_cols[c] + NKV) * PW] for c in range(1, 6)]
            tail += [w[:, :, i * PW:(i + 1) * PW] for i in range(NKV) for w in (w_co, w_ao)]
            tail += [w_o[:, :, i * PW:(i + 1) * PW] for i in range(NKV)]
            for src in tail:
                slot_split(n)
                load1(n % RING1, src)
                n += 1

            def load_bias(e, par):
                for m, name in enumerate(("b_up", "b_gate")):
                    sp.dma_start(brow[32 * par:32 * par + 1, m * D:(m + 1) * D],
                                 A[name][0, bass.ds(e, 1), :]).then_inc(bias_full[par], 16)

            def load_expert(e, c, wait):
                for r in range(EP):
                    s = phys((c * EP + r) % RING)
                    wait(r, s)
                    k = 2 * (r % 4)
                    sp.dma_start(ring[:, s, :].rearrange("p (k n) -> p k n", k=2),
                                 experts[r // 4][bass.ds(e, 1), :, k:k + 2, :].rearrange("a p k n -> p (a k) n"),
                                 ).then_inc(slot_full[s], 16)

            def expert_turn(it, first):
                for c in range(UNROLL):
                    if not (first and c < 2):
                        sp.wait_ge(weights_used, it * (UNROLL * EP) + ((c - 2) * EP + 8))
                    load_bias(it * UNROLL + c, c % 2)

                    def wait(r, s):
                        p = c * EP + r
                        if not (first and p < RING):
                            sp.wait_ge(weights_used, it * (UNROLL * EP) + (p + 1 - RING))
                        elif s < RING1:
                            slot_split(max(n for n in range(NP1) if n % RING1 == s) + RING1)
                        elif s < 12:
                            sp.wait_ge(blocks_done, 2 * (NIN + 2 * NKV))
                            sp.wait_ge(merged_ready, NKV)
                        else:
                            sp.wait_ge(blocks_done, 2 * NP1)
                    load_expert(it * UNROLL + c, c, wait)

            expert_turn(0, True)
            with sp.Fori(1, NE // UNROLL) as it:
                expert_turn(it, False)

            sp.wait_ge(nov_ready, 1)
            nov = sp.value_load(novt[0:1, 0:1], min_val=0, max_val=NJ)
            with sp.If(nov > 0):
                sp.wait_ge(ov_dve, 3)
                with sp.Fori(0, nov) as j:
                    sp.wait_ge(scattered, j + (NE + 1))
                    e = sp.value_load(eid[0:1, bass.ds(j, 1)], min_val=0, max_val=NE - 1)
                    load_bias(e, 0)
                    load_expert(e, 0, lambda r, s: None)
            sp.wait_ge(out_ready, 2)
            sp.dma_start(out[0].rearrange("(t p) d -> p t d", p=P), normed[:, :, :]).then_inc(out_done, 16)
            sp.wait_ge(out_done, 16)

        @block.tensor
        def _(pe):
            def bank(b, lo=0, n=512):
                return psum[:, b, lo:lo + n]

            def project_T(b, n, par, src):
                high, low = src
                for m in range(2):
                    pe.wait_ge((wL0_ready, wL1_ready)[m], n + 1)
                    for k in range(KB):
                        for w, x in ((wH, low), (wH, high), (wL, high)):
                            mm = pe.matmul(bank(b, m * T, T), w[:, par, m, k, :], x[:, k, :],
                                           start=(k == 0 and x is low), stop=(k == KB - 1 and w is wL))
                    mm.then_inc(blocks_done, 1)

            def project(b, n, par, src):
                high, low = src
                pe.wait_ge(wL0_ready, n + 1)
                pe.wait_ge(wL1_ready, n + 1)
                for t in range(TT):
                    for k in range(KB):
                        for x, w in ((low, wH), (high, wH), (high, wL)):
                            mm = pe.matmul(bank(b, t * PW, PW).rearrange("p (m n) -> p m n", m=2),
                                           x[:, k, t * P:(t + 1) * P], w[:, par, :, k, :],
                                           start=(k == 0 and x is low), stop=(k == KB - 1 and w is wL))
                mm.then_inc(blocks_done, 2)

            def turn_normed(done):
                for k in range(KB):
                    for t in range(TT):
                        tr = pe.transpose(bank(3 + k // 2, (k % 2) * T + t * P, P), normed[:, t, k * P:(k + 1) * P], ident)
                    if k % 2:
                        tr.then_inc(done, 1)

            pe.wait_ge(cst_in, 16)
            pe.wait_ge(par_in, 48)
            pe.transpose(bank(7, 0, 84), params[:, :], ident[0:84, 0:84]).then_inc(par_turned, 1)
            pe.wait_ge(normed_ready, 2)
            turn_normed(x_turned)

            pe.wait_ge(par_ready, 1)
            pe.wait_ge(hT_ready, KB)
            project_T(7, 0, 0, (hH, hL))
            project(6, 1, 1, (hH, hL))
            with pe.Fori(0, NKV) as i:
                project_T(2, i * 6 + 2, 0, (hH, hL))
                project_T(0, i * 6 + 3, 1, (hH, hL))
                pe.wait_ge(rotated, i + 2)
                pe.wait_ge(kz_ready, 9)
                for m in range(2):
                    pe.matmul(psum[:, 3, m * 256:(m + 1) * 256].rearrange("p (h s) -> p h s", h=2), q[:, m, 0:P],
                              kz[:, bass.ds(i, 1), :, 0:P].rearrange("p a h s -> p (a h) s"), start=True, stop=True)
                for m in range(2):
                    mm = pe.matmul(psum[:, 4 + m, :].rearrange("p (h s) -> p h s", h=2), q[:, m, P:2 * P],
                                   kz[:, bass.ds(i, 1), :, :].rearrange("p a h s -> p (a h) s"), start=True, stop=True)
                mm.then_inc(scores_ready, 1)
                project_T(1, i * 6 + 4, 0, (hH, hL))
                pe.wait_ge(raw_ready, i + 2)
                project_T(2, i * 6 + 5, 1, (hH, hL))
                pe.wait_ge(cc_ready, i + 1)
                project_T(0, i * 6 + 6, 0, (hH, hL))
                pe.wait_ge(p_ready, i + 1)
                for h in range(4):
                    pe.transpose(bank(3, h * P, P), sm[:, h * P:(h + 1) * P], ident)
                for n in range(8):
                    tr = pe.transpose(bank(4 + n // 4, (n % 4) * P, P), sm[:, 512 + n * P:512 + (n + 1) * P], ident)
                tr.then_inc(pT_turned, 1)
                pe.wait_ge(u_ready, i + 1)
                project_T(1, i * 6 + 7, 1, (hH, hL))
                pe.wait_ge(vcur_ready, i + 1)
                pe.wait_ge(pT_ready, i * 2 + 2)
                pe.wait_ge(bank6_read, i + 1)
                o = psum[:, 6, :].rearrange("p (m t s) -> p m t s", m=2, t=TT)
                for h in range(2):
                    pe.matmul(o[64 * h:64 * h + 64, :, 0, :], vcur[:, 0, :], pT[:, h:4:2, :], start=True, stop=True,
                              tile_position=(0, 64 * h))
                for kb in range(2):
                    for h in range(2):
                        mm = pe.matmul(o[64 * h:64 * h + 64, :, 1, :], vcur[:, kb, :],
                                       pT[:, 4 + 2 * h + kb:4 + 2 * h + kb + 5:4, :], start=(kb == 0), stop=(kb == 1),
                                       tile_position=(0, 64 * h))
                mm.then_inc(o_ready, 1)
                pe.wait_ge(z_ready, i + 1)
                pe.wait_ge(gates_ready, i * 2 + 2)

            n = NIN
            for i in range(NKV):
                for src in ((zH, zL), (aH, aL)):
                    if n >= NIN + 3:
                        pe.wait_ge(branch_read, n - NIN - 2)
                    if i == 0 and src[0] is zH:
                        pe.wait_ge(zL_ready, NKV)
                    elif i == 0:
                        pe.wait_ge(bank6_read, NKV + 1)
                    project_T(n % 3, n, n % 2, src)
                    n += 1
            pe.wait_ge(merged_ready, NKV)
            for i in range(NKV):
                if i == 3:
                    pe.wait_ge(x1_ready, 1)
                project(n % 3, n, n % 2, (mH, mL))
                n += 1

            pe.wait_ge(normed_ready, 4)
            turn_normed(h2T_turned)
            pe.wait_ge(small_in, 16 * 5)
            pe.wait_ge(h2T_ready, 4)
            for t in range(TT):
                for k in range(KB):
                    mm = pe.matmul(bank(7, t * NE, NE), mt[:, k, t * P:(t + 1) * P], wr[:, k, :],
                                   start=(k == 0), stop=(k == KB - 1))
            mm.then_inc(logits_ready, 1)
            pe.wait_ge(M_ready, 1)
            one16, tr16 = tri16[:, P:2 * P], tri16[:, 0:P]
            pe.matmul(bank(7, 64, NE), tr16, Mb[:, 0, :], start=True, stop=True)
            pe.matmul(bank(7, 96, NE), one16, Mb[:, 0, :], start=True, stop=False)
            pe.matmul(bank(7, 96, NE), tr16, Mb[:, 1, :], start=False, stop=True)
            pe.matmul(bank(7, 128, NE), one16, Mb[:, 0, :], start=True, stop=False)
            pe.matmul(bank(7, 128, NE), one16, Mb[:, 1, :], start=False, stop=True).then_inc(ranks_ready, 1)

            def gather(nth):
                pe.wait_ge(G_ready, nth + 1)
                for k in range(KB):
                    for t in range(TT):
                        for part in range(3):
                            mm = pe.matmul(bank(6, k * CW, CW), h2b[:, part, t, k * P:(k + 1) * P], G[:, t, :],
                                           start=(t == 0 and part == 0), stop=(t == TT - 1 and part == 2))
                mm.then_inc(gathered, 1)

            def wide(b, src, c, first_r, uses, bias):
                if bias is not None:
                    par, m = bias
                    for h in range(2):
                        pe.matmul(psum[64 * h:64 * h + 64, b, :], cst[32 * par:32 * par + 1, C_ONE:C_ONE + CW],
                                  brow[32 * par:32 * par + 1, m * D + h * 512:m * D + (h + 1) * 512],
                                  start=True, stop=False, tile_position=(32 * par, 64 * h))
                for r in range(first_r, first_r + 4):
                    s = phys((c * EP + r) % RING)
                    pe.wait_ge(slot_full[s], uses(s, c * EP + r))
                    w = ring[:, s, :].rearrange("p (k n) -> p k n", k=2)
                    for k2 in range(2):
                        k = 2 * (r % 4) + k2
                        for h in range(2):
                            mm = pe.matmul(psum[64 * h:64 * h + 64, b, :], src[:, k, :], w[:, k2, h * 512:(h + 1) * 512],
                                           start=(bias is None and k == 0), stop=(k == KB - 1),
                                           tile_position=(0, 64 * h))
                    mm.then_inc(weights_used, 1)

            def scatter(nth, chunk):
                pe.wait_ge(ysb_ready, chunk + 1)
                pe.wait_ge(S_ready, chunk + 1)
                for t in range(TT):
                    for h in range(2):
                        mm = pe.matmul(bank(2 * t + h), S[64 * h:64 * h + 64, t * P:(t + 1) * P],
                                       ysb[64 * h:64 * h + 64, :], start=False, stop=False, skip_group_check=True,
                                       tile_position=(64 * h, 0))
                mm.then_inc(scattered, 1)

            def turn_weights(j):
                pe.wait_ge(Gw_ready, j + 1)
                for t in range(TT):
                    tr = pe.transpose(bank(4, t * P, P), Gw[:, t, :, :].rearrange("p h c -> p (h c)"), ident)
                tr.then_inc(S_turned, 1)

            def turn_act(j):
                pe.wait_ge(act_ready, j + 1)
                for b in range(4):
                    tr = pe.transpose(bank(5, b * P, P), act[:, b * P:(b + 1) * P], ident)
                tr.then_inc(act_turned, 1)

            pe.wait_ge(part_ready, 3)
            pe.wait_ge(h2T_ready, 4)
            gather(0)
            pe.wait_ge(wgt_ready, 1)
            for t in range(TT):
                tr = pe.transpose(psum[0:NE, 5, t * P:(t + 1) * P], wgt[:, t, 0:NE], ident)
            tr.then_inc(wT_turned, 1)
            pe.wait_ge(wT_ready, 1)
            pe.wait_ge(bdn_in, 16)
            pe.wait_ge(x1_ready, NKV)
            for t in range(TT):
                for h in range(2):
                    pe.matmul(bank(2 * t + h), wT[:, t * P:(t + 1) * P], bdn[:, h * 512:(h + 1) * 512], start=True,
                              stop=False, skip_group_check=True)
            with pe.Fori(0, NE // UNROLL) as it:
                def uses(s, p):
                    return it * (16 * UNROLL * EP // RING) + 16 * (uses1(s) + p // RING + 1)
                for c in range(UNROLL):
                    j = it * UNROLL + c
                    pe.wait_ge(bias_full[c % 2], it * (32 * UNROLL // 2) + 32 * (c // 2 + 1))
                    pe.wait_ge(xe_ready, j + 1)
                    pe.wait_ge(S_ready, j + 1)
                    wide(4, xe, c, 0, uses, (c % 2, 0))
                    wide(5, xe, c, 4, uses, (c % 2, 1))
                    scatter(j, j)
                    gather(j + 1)
                    turn_act(j)
                    turn_weights(j)
                    pe.wait_ge(aT_ready, j + 1)
                    wide(7, aT, c, 8, uses, None)
            scatter(NE, NE)

            pe.wait_ge(nov_ready, 1)
            nov = pe.value_load(novt[0:1, 0:1], min_val=0, max_val=NJ)
            with pe.If(nov > 0):
                for t in range(TT):
                    pe.transpose(psum[0:NE, 6, t * P:(t + 1) * P], pos[:, t, 0:NE], ident)
                for t in range(TT):
                    mm = pe.matmul(psum[0:NE, 6, 256:257], Mf[:, t, :], cst[:, C_ONE:C_ONE + 1], start=(t == 0),
                                   stop=(t == TT - 1))
                mm.then_inc(ov_pe, 1)
                pe.wait_ge(ov_dve, 1)
                pe.matmul(psum[0:NE, 6, 300:301], tri[0:NE, 0:NE], ovn, start=True, stop=True).then_inc(ov_pe, 1)
                pe.wait_ge(ov_dve, 2)
                pe.matmul(psum[0:1, 6, 320:320 + NJ], cst[0:NE, C_COL:C_COL + 1], ovE, start=True, stop=True)
                for t in range(TT):
                    pe.matmul(bank(6, 352 + t * NJ, NJ), wT[:, t * P:(t + 1) * P], ovE, start=True, stop=True)
                for t in range(TT):
                    pe.matmul(bank(6, 352 + (2 + t) * NJ, NJ), posT[:, t * P:(t + 1) * P], ovE, start=True, stop=False)
                    mm = pe.matmul(bank(6, 352 + (2 + t) * NJ, NJ), ones[0:NE, :], ovK, start=False, stop=True)
                mm.then_inc(ov_pe, 1)
                with pe.Fori(0, nov) as j:
                    def uses(s, p):
                        return j * 16 + 16 * (uses1(s) + NE * EP // RING + 1)
                    gather(j + (NE + 1))
                    pe.wait_ge(bias_full[0], j * 32 + 32 * (NE // 2 + 1))
                    pe.wait_ge(xe_ready, j + (NE + 2))
                    wide(4, xe, 0, 0, uses, (0, 0))
                    wide(5, xe, 0, 4, uses, (0, 1))
                    turn_act(j + NE)
                    turn_weights(j + NE)
                    pe.wait_ge(aT_ready, j + (NE + 1))
                    wide(7, aT, 0, 8, uses, None)
                    scatter(j + (NE + 1), j + (NE + 1))

        @block.scalar
        def _(act_e):
            act_e.dma_start(cst[:, :], A["constants"]).then_inc(cst_in, 16)
            act_e.dma_start(params[0:8, :], A["g_mix"][0].rearrange("(r c) -> r c", c=P)).then_inc(par_in, 16)
            act_e.dma_start(params[8:60, :], A["b_in"][0].rearrange("(r c) -> r c", c=P)).then_inc(par_in, 16)
            act_e.dma_start(params[60:84, :], A["w_conv"][0].rearrange("j (r c) -> (j r) c", c=P)).then_inc(par_in, 16)
            act_e.dma_start(bv, A["b_in"][0:1, VCOL * PW:(VCOL + 1) * PW].partition_broadcast(P)).then_inc(small_in, 16)
            act_e.dma_start(snk[:, :], A["sinks"][0:1, :].partition_broadcast(P)).then_inc(small_in, 16)
            act_e.dma_start(gbc[:, :], A["g_ffn"][0:1, :].partition_broadcast(P)).then_inc(small_in, 16)
            act_e.dma_start(wr[:, :, :], A["w_router"][0].rearrange("(k p) e -> p k e", p=P)).then_inc(small_in, 16)
            act_e.dma_start(brt[:, :], A["b_router"][0:1, :].partition_broadcast(P)).then_inc(small_in, 16)

            def square_sums(col):
                for t in range(TT):
                    nc.scalar.activation(normed[:, t, :], xres[:, t, :], ACT.Square,
                                         accum_out=small[:, col + t:col + t + 1]).then_inc(ssq_ready, 1)

            def split_high(n, s, uses, par, fresh=False):
                act_e.wait_ge(slot_full[s], uses)
                for m in range(2):
                    if not fresh:
                        act_e.wait_ge(blocks_done, n * 2 + (m - 3))
                    nc.scalar.copy(wH[:, par, m, :, :],
                                   ring[:, s, :].rearrange("p (k n) -> p k n", k=KB)[:, :, m * P:(m + 1) * P],
                                   ).then_inc(wH_ready, 1)

            def split_high_in_turn(i, c):
                split_high(i * 6 + (2 + c), (2 + c) % RING1, i * 32 + 16 * ((2 + c) // RING1 + 1), c % 2)

            act_e.wait_ge(x_in, 16)
            square_sums(0)
            split_high(0, 0, 16, 0, fresh=True)
            act_e.wait_ge(par_ready, 1)
            for k in range(KB):
                act_e.wait_ge(x_turned, k // 2 + 1)
                nc.scalar.activation(hH[:, k, :], psum[:, 3 + k // 2, (k % 2) * T:(k % 2 + 1) * T], ACT.Copy,
                                     scale=g1T[:, k:k + 1]).then_inc(hH_ready, 1)
            split_high(1, 1, 16, 1, fresh=True)
            split_high(2, 2, 16, 0)
            act_e.wait_ge(blocks_done, 2)
            for b in range(2):
                ins = nc.scalar.activation(raw[:, b, :], psum[:, 7, b * T:(b + 1) * T], ACT.Identity,
                                           bias=bT[:, 2 * KCOL + b:2 * KCOL + b + 1])
            ins.then_inc(raw_ready, 1)

            act_e.wait_ge(kz_ready, 1)
            act_e.wait_ge(rotated, 1)
            for kv in range(NKV):
                a = 64 * (kv % 2)
                for h in range(2):
                    nc.scalar.copy(kz[64 * h:64 * h + 64, kv, h, :], kT[a:a + 64, kv // 2, :]).then_inc(kz_ready, 1)

            with act_e.Fori(0, NKV) as i:
                split_high_in_turn(i, 1)
                act_e.wait_ge(blocks_done, i * 12 + 6)
                act_e.wait_ge(rotated, i + 1)
                for b in range(2):
                    ins = nc.scalar.activation(raw[:, b, :], psum[:, 2, b * T:(b + 1) * T], ACT.Identity,
                                               bias=bT[:, bass.ds(i * 2 + b, 1)])
                ins.then_inc(raw_ready, 1)
                split_high_in_turn(i, 2)
                act_e.wait_ge(blocks_done, i * 12 + 8)
                for b in range(2):
                    ins = nc.scalar.activation(ccs[:, b, :], psum[:, 0, b * T:(b + 1) * T], ACT.Identity,
                                               bias=bT[:, bass.ds(i * 2 + (2 * CC + b), 1)])
                ins.then_inc(cc_ready, 1)
                split_high_in_turn(i, 3)
                split_high_in_turn(i, 4)
                act_e.wait_ge(max_ready, i + 1)
                nc.scalar.activation(small[:, 32:40], small[:, 32:40], ACT.Exp)
                for t in range(TT):
                    for h in range(4):
                        n, at = t * 4 + h, (h * P, 512 + h * T)[t]
                        s = sm[:, at:at + (t + 1) * P]
                        ins = nc.scalar.activation(s, s, ACT.Exp, bias=small[:, 16 + n:17 + n],
                                                   accum_out=small[:, 24 + n:25 + n])
                ins.then_inc(exp_ready, 1)
                split_high_in_turn(i, 5)
                act_e.wait_ge(z_ready, i + 1)
                nc.scalar.copy(zH[:, bass.ds(i * 2, 2), :], ycv).then_inc(zH_ready, 1)
                for which, b, col, due in ((ga, 0, GA, 7), (gc, 1, GC, 8)):
                    act_e.wait_ge(blocks_done, i * 12 + 2 * due)
                    for m in range(2):
                        ins = nc.scalar.activation(which[:, bass.ds(i * 2 + m, 1), :].rearrange("p a t -> p (a t)"),
                                                   psum[:, b, m * T:(m + 1) * T], ACT.Sigmoid,
                                                   bias=bT[:, bass.ds(i * 2 + (2 * col + m), 1)])
                    ins.then_inc(gates_ready, 1)
                    if which is ga:
                        split_high_in_turn(i, 6)
                        act_e.wait_ge(pT_turned, i + 1)
                        nc.scalar.copy(pT[:, 0:4, :].rearrange("p n q -> p (n q)"), psum[:, 3, :]).then_inc(pT_ready, 1)
                        nc.scalar.copy(pT[:, 4:12, :].rearrange("p n q -> p (n q)"),
                                       psum[:, 4:6, :].rearrange("p b n -> p (b n)")).then_inc(pT_ready, 1)
                act_e.wait_ge(o_ready, i + 1)
                nc.scalar.copy(aH[:, bass.ds(i * 2, 2), :].rearrange("p m t -> p (m t)"),
                               psum[:, 6, :]).then_inc(aH_ready, 1)
                act_e.wait_ge(u_ready, i + 1)

            for n in range(NIN, NP1):
                if n + 1 < NP1:
                    split_high(n + 1, (n + 1) % RING1, 16 * ((n + 1) // RING1 + 1), (n + 1) % 2)
                i, second = (n - NIN) // 2, (n - NIN) % 2
                if second and i < NKV:
                    act_e.wait_ge(msum_ready, i + 1)
                    nc.scalar.copy(mH[:, 2 * i:2 * i + 2, :], raw).then_inc(mH_ready, 1)
            act_e.wait_ge(merged_ready, NKV)
            act_e.dma_start(bdn, A["b_down"][0]).then_inc(bdn_in, 16)
            act_e.wait_ge(x1_ready, NKV)
            square_sums(6)
            act_e.wait_ge(normed_ready, 4)
            for b in range(4):
                act_e.wait_ge(h2T_turned, b + 1)
                nc.scalar.copy(mt[:, 2 * b:2 * b + 2, :].rearrange("p k t -> p (k t)"), psum[:, 3 + b, :]).then_inc(h2T_ready, 1)
            nc.scalar.copy(h2b[:, 0, :, :], normed[:, :, :]).then_inc(part_ready, 1)
            act_e.dma_start(gbc[:, :], A["g_final"].rearrange("(a d) -> a d", a=1).partition_broadcast(P)).then_inc(gfin_in, 16)
            act_e.wait_ge(shifted_ready, 1)
            nc.scalar.activation(topw, topw, ACT.Exp).then_inc(topexp_ready, 1)
            act_e.wait_ge(rest_ready, 1)
            nc.scalar.copy(h2b[:, 1, :, :], normed[:, :, :]).then_inc(part_ready, 1)

            def take_gathered(nth):
                act_e.wait_ge(gathered, nth + 1)
                nc.scalar.copy(xe.rearrange("p k c -> p (k c)"), psum[:, 6, :]).then_inc(xe_ready, 1)

            def take_act(j):
                act_e.wait_ge(act_turned, j + 1)
                nc.scalar.copy(aT.rearrange("p (h b) c -> p b h c", h=2),
                               psum[:, 5, :].rearrange("p (b h c) -> p b h c", b=4, h=2)).then_inc(aT_ready, 1)

            def take_y(used):
                act_e.wait_ge(weights_used, used)
                nc.scalar.copy(ysb, psum[:, 7, :]).then_inc(ysb_ready, 1)

            def squash(j):
                act_e.wait_ge(gmin_ready, j + 1)
                nc.scalar.activation(sg, gm, ACT.Sigmoid, scale=ALPHA).then_inc(sig_ready, 1)

            act_e.wait_ge(ysb_ready, 1)
            take_gathered(0)
            act_e.wait_ge(wT_turned, 1)
            nc.scalar.copy(wT[:, :], psum[0:NE, 5, 0:256]).then_inc(wT_ready, 1)
            with act_e.Fori(0, NE // UNROLL) as it:
                for c in range(UNROLL):
                    j = it * UNROLL + c
                    squash(j)
                    take_gathered(j + 1)
                    take_act(j)
                    take_y(it * (UNROLL * EP) + (c + 1) * EP)
            act_e.wait_ge(nov_ready, 1)
            nov = act_e.value_load(novt[0:1, 0:1], min_val=0, max_val=NJ)
            with act_e.If(nov > 0):
                with act_e.Fori(0, nov) as j:
                    take_gathered(j + (NE + 1))
                    squash(j + NE)
                    take_act(j + NE)
                    take_y(j * EP + (NE + 1) * EP)
            act_e.wait_ge(x2_ready, 1)
            square_sums(48)

        @block.vector
        def _(dve):
            v = nc.vector
            steps = Steps(dve, dve_step)

            def ms(col):
                v.tensor_scalar(small[:, col + 2:col + 4], small[:, col:col + 2], 1.0 / D, EPS, ALU.mult,
                                ALU.add).then_inc(ms_ready, 1)

            def rotate(dst):
                for quarter in range(4):
                    a, b = 32 * quarter, 32 * (quarter ^ 1)
                    ins = v.tensor_copy(swp[a:a + 32, :, :], raw[b:b + 32, :, :])
                steps.link(ins)
                cos = cst[:, C_COS:C_COS + T].unsqueeze(1).broadcast_to([P, 2, T])
                sin = cst[:, C_SIN:C_SIN + T].unsqueeze(1).broadcast_to([P, 2, T])
                v.tensor_tensor(dst, raw, cos, ALU.mult)
                steps.link(v.tensor_tensor(swp, swp, sin, ALU.mult))
                v.tensor_tensor(dst, dst, swp, ALU.add).then_inc(rotated, 1)

            def split_low(n, par):
                dve.wait_ge(wH_ready, n * 2 + 2)
                s = (n if isinstance(n, int) else par[0]) % RING1
                p2 = n % 2 if isinstance(n, int) else par[1]
                v.tensor_tensor(wL[:, p2, 1, :, :], ring[:, s, :].rearrange("p (k n) -> p k n", k=KB)[:, :, P:2 * P],
                                wH[:, p2, 1, :, :].bitcast(F32), ALU.subtract).then_inc(wL1_ready, 1)

            def split_low_in_turn(i, c):
                split_low(i * 6 + (2 + c), (2 + c, c % 2))

            dve.wait_ge(cst_in, 16)
            v.memset(u[:, :, 0:2], 0.0)
            v.memset(pos[:, :, NE:NE + 1], NEVER)
            v.memset(wgt[:, :, NE:NE + 1], 0.0)
            steps.link(v.tensor_copy(tri16[:, :], cst[:, C_TRI:C_TRI + 2 * P]))
            dve.wait_ge(ssq_ready, 2)
            ms(0)
            dve.wait_ge(rstd_ready, 1)
            for t in range(TT):
                v.tensor_scalar(normed[:, t, :], xres[:, t, :], small[:, 4 + t:5 + t], None, ALU.mult).then_inc(normed_ready, 1)
            dve.wait_ge(par_turned, 1)
            v.tensor_copy(parT[:, :], psum[:, 7, 0:84]).then_inc(par_ready, 1)
            dve.wait_ge(par_ready, 1)
            for k in range(KB):
                dve.wait_ge(hH_ready, 2 * (k // 2) + 2)
                v.scalar_tensor_tensor(hL[:, k, :], psum[:, 3 + k // 2, (k % 2) * T:(k % 2 + 1) * T], g1T[:, k:k + 1],
                                       hH[:, k, :].bitcast(F32), ALU.mult, ALU.subtract).then_inc(hT_ready, 1)
                if k == 1:
                    split_low(0, None)
            split_low(1, None)
            split_low(2, None)
            dve.wait_ge(raw_ready, 1)
            rotate(kT)
            dve.wait_ge(blocks_done, 4)
            dve.wait_ge(small_in, 16 * 5)
            v.tensor_tensor(V, psum[:, 6, :].rearrange("p (t c) -> p t c", t=TT), bv.unsqueeze(1).broadcast_to([P, TT, PW]),
                            ALU.add).then_inc(bank6_read, 1)

            with dve.Fori(0, NKV) as i:
                steps.begin_loop(i, 10)
                split_low_in_turn(i, 1)
                dve.wait_ge(raw_ready, i + 2)
                rotate(q)
                split_low_in_turn(i, 2)
                dve.wait_ge(scores_ready, i + 1)
                s0 = sm[:, 0:512].rearrange("p (h s) -> p h s", h=4)
                s1 = sm[:, 512:1536].rearrange("p (h s) -> p h s", h=4)
                v.scalar_tensor_tensor(s0, psum[:, 3, :].rearrange("p (h s) -> p h s", h=4), HD ** -0.5,
                                       cst[:, C_M0:C_M0 + P].unsqueeze(1).broadcast_to([P, 4, P]), ALU.mult, ALU.add)
                steps.link(v.scalar_tensor_tensor(
                    s1, psum[:, 4:6, :].rearrange("p b (h s) -> p (b h) s", h=2), HD ** -0.5,
                    cst[:, C_M1:C_M1 + T].unsqueeze(1).broadcast_to([P, 4, T]), ALU.mult, ALU.add))
                v.tensor_reduce(small[:, 8:12], s0, AX.X, ALU.max)
                steps.link(v.tensor_reduce(small[:, 12:16], s1, AX.X, ALU.max))
                mx = small[:, 8:16].rearrange("p (t h) -> p t h", t=TT)
                sink = snk[:, bass.ds(i * 4, 4)].unsqueeze(1).broadcast_to([P, TT, 4])
                steps.link(v.tensor_tensor(mx, mx, sink, ALU.max))
                v.tensor_tensor(small[:, 32:40].rearrange("p (t h) -> p t h", t=TT), sink, mx, ALU.subtract)
                v.tensor_scalar(small[:, 16:24], small[:, 8:16], -1.0, None, ALU.mult).then_inc(max_ready, 1)
                split_low_in_turn(i, 3)
                dve.wait_ge(blocks_done, i * 12 + 10)
                dve.wait_ge(cc_ready, i + 1)
                for b in range(2):
                    ins = v.scalar_tensor_tensor(u[:, b, 2:T + 2], psum[:, 1, b * T:(b + 1) * T],
                                                 bT[:, bass.ds(i * 2 + (2 * CX + b), 1)], ccs[:, b, :], ALU.add, ALU.mult)
                ins.then_inc(u_ready, 1)
                split_low_in_turn(i, 4)
                dve.wait_ge(u_ready, i + 1)
                for tap in range(3):
                    for b in range(2):
                        w = wcT[:, bass.ds(i * 2 + (8 * tap + b), 1)]
                        if tap == 0:
                            ins = v.tensor_scalar(ycv[:, b, :], u[:, b, 0:T], w, None, ALU.mult)
                        else:
                            ins = v.scalar_tensor_tensor(ycv[:, b, :], u[:, b, tap:tap + T], w, ycv[:, b, :], ALU.mult, ALU.add)
                    steps.link(ins)
                dve.wait_ge(exp_ready, i + 1)
                steps.link(v.tensor_tensor(small[:, 24:32], small[:, 24:32], small[:, 32:40], ALU.add))
                steps.link(v.reciprocal(small[:, 40:48], small[:, 24:32]))
                v.tensor_tensor(s0, s0, small[:, 40:44].unsqueeze(2).broadcast_to([P, 4, P]), ALU.mult)
                v.tensor_tensor(s1, s1, small[:, 44:48].unsqueeze(2).broadcast_to([P, 4, T]), ALU.mult).then_inc(p_ready, 1)
                dve.wait_ge(blocks_done, i * 12 + 12)
                for b in range(2):
                    ins = v.scalar_tensor_tensor(ycv[:, b, :],
                                                 psum[:, 2, b * T:(b + 1) * T], bT[:, bass.ds(i * 2 + (2 * CB + b), 1)],
                                                 ycv[:, b, :], ALU.add, ALU.mult)
                ins.then_inc(z_ready, 1)
                split_low_in_turn(i, 5)
                split_low_in_turn(i, 6)
                dve.wait_ge(pT_turned, i + 1)
                dve.wait_ge(aH_ready, i + 1)
                v.tensor_tensor(aL[:, bass.ds(i * 2, 2), :].rearrange("p m t -> p (m t)"), psum[:, 6, :],
                                aH[:, bass.ds(i * 2, 2), :].rearrange("p m t -> p (m t)").bitcast(F32),
                                ALU.subtract).then_inc(bank6_read, 1)
                dve.wait_ge(zL_ready, i + 1)
                steps.end_loop(NKV)

            dve.wait_ge(gates_ready, 2 * NKV)
            n = NIN
            flat = lambda x: x.rearrange("p m t -> p (m t)")
            for i in range(NKV):
                if i:
                    dve.wait_ge(merged_ready, i)
                for gate, tmp in ((gc, raw), (ga, swp)):
                    split_low(n + 1, None)
                    dve.wait_ge(blocks_done, 2 * (n + 1))
                    v.tensor_tensor(flat(tmp), psum[:, n % 3, :], flat(gate[:, 2 * i:2 * i + 2, :]), ALU.mult).then_inc(branch_read, 1)
                    n += 1
                dve.wait_ge(branch_read, 2 * (i + 1))
                v.tensor_tensor(raw, raw, swp, ALU.add).then_inc(msum_ready, 1)
                dve.wait_ge(mH_ready, i + 1)
                v.tensor_tensor(mL[:, 2 * i:2 * i + 2, :], raw, mH[:, 2 * i:2 * i + 2, :].bitcast(F32),
                                ALU.subtract).then_inc(merged_ready, 1)
            dve.wait_ge(merged_ready, NKV)
            v.memset(S, 0.0).then_inc(S_ready, 1)
            v.memset(ysb, 0.0).then_inc(ysb_ready, 1)
            for i in range(NKV):
                if n + 1 < NP1:
                    split_low(n + 1, None)
                dve.wait_ge(blocks_done, 2 * (n + 1))
                xs = xres[:, :, i * PW:(i + 1) * PW]
                v.tensor_tensor(xs, psum[:, n % 3, :].rearrange("p (t c) -> p t c", t=TT), xs, ALU.add).then_inc(x1_ready, 1)
                n += 1
            dve.wait_ge(ssq_ready, 4)
            ms(6)
            dve.wait_ge(rstd_ready, 2)
            for t in range(TT):
                v.scalar_tensor_tensor(normed[:, t, :], xres[:, t, :], small[:, 10 + t:11 + t], gbc[:, :], ALU.mult,
                                       ALU.mult).then_inc(normed_ready, 1)

            dve.wait_ge(logits_ready, 1)
            steps.link(v.tensor_tensor(lg, psum[:, 7, 0:2 * NE].rearrange("p (t e) -> p t e", t=TT),
                                       brt[:, :].unsqueeze(1).broadcast_to([P, TT, NE]), ALU.add))
            for t in range(TT):
                ins = v.max(top8[:, t, :], lg[:, t, :])
            steps.link(ins)
            v.tensor_tensor(topw, top8[:, :, 0:TOPK], top8[:, :, 0:1].broadcast_to([P, TT, TOPK]),
                            ALU.subtract).then_inc(shifted_ready, 1)
            for t in range(TT):
                ins = v.max_index(topi[:, t, :], top8[:, t, :], lg[:, t, :])
            steps.link(ins)
            steps.link(v.tensor_copy(topf, topi[:, :, :]))
            for t in range(TT):
                ins = v.tensor_tensor(onehot[:, t], count_up[:, 0:NE].unsqueeze(1).broadcast_to([P, TOPK, NE]),
                                      topf[:, t, 0:TOPK].unsqueeze(2).broadcast_to([P, TOPK, NE]), ALU.is_equal)
            steps.link(ins)
            for t in range(TT):
                ins = v.tensor_reduce(Mf[:, t, :], onehot[:, t].rearrange("p k e -> p e k"), AX.X, ALU.add)
            steps.link(ins)
            v.tensor_copy(Mb[:, :, :], Mf[:, :, :]).then_inc(M_ready, 1)
            dve.wait_ge(topexp_ready, 1)
            steps.link(v.tensor_reduce(tops, topw, AX.X, ALU.add))
            steps.link(v.reciprocal(tops, tops))
            steps.link(v.tensor_tensor(topw, topw, tops.unsqueeze(2).broadcast_to([P, TT, TOPK]), ALU.mult))
            for t in range(TT):
                ins = v.tensor_tensor(onehot[:, t], onehot[:, t], topw[:, t, :].unsqueeze(2).broadcast_to([P, TOPK, NE]),
                                      ALU.mult)
            steps.link(ins)
            for t in range(TT):
                ins = v.tensor_reduce(wgt[:, t, 0:NE], onehot[:, t].rearrange("p k e -> p e k"), AX.X, ALU.add)
            ins.then_inc(wgt_ready, 1)
            dve.wait_ge(ranks_ready, 1)
            steps.link(v.scalar_tensor_tensor(pos[:, :, 0:NE], psum[:, 7, 64:128].rearrange("p (t e) -> p t e", t=TT),
                                              -NEVER, Mf[:, :, :], ALU.add, ALU.mult))
            steps.link(v.tensor_scalar(pos[:, :, 0:NE], pos[:, :, 0:NE], NEVER, None, ALU.add))

            def one_hot(nth, table, at):
                if not isinstance(nth, int):
                    dve.wait_ge(gathered, nth)
                for t in range(TT):
                    ins = v.tensor_scalar(G[:, t, :], iota, table[:, t, at], None, ALU.is_equal)
                ins.then_inc(G_ready, 1)

            def one_hot_weights(j, table, weights, at):
                for t in range(TT):
                    ins = v.tensor_scalar(Gw[:, t, :, :], iota.unsqueeze(1).broadcast_to([P, 2, CW]), table[:, t, at],
                                          weights[:, t, at], ALU.is_equal, ALU.mult)
                ins.then_inc(Gw_ready, 1)

            def swiglu(j, used):
                dve.wait_ge(weights_used, used + 4)
                v.tensor_scalar(uc, psum[:, 4, :], LIMIT, -LIMIT, ALU.min, ALU.max)
                dve.wait_ge(weights_used, used + 8)
                v.tensor_scalar(gm, psum[:, 5, :], LIMIT, None, ALU.min).then_inc(gmin_ready, 1)
                dve.wait_ge(gmin_ready, j + 1)
                v.scalar_tensor_tensor(uc, uc, 1.0, gm, ALU.add, ALU.mult)
                dve.wait_ge(sig_ready, j + 1)
                steps.link(v.tensor_copy(small[:, 60:61], small[:, 0:1]))
                v.tensor_tensor(act, uc, sg, ALU.mult).then_inc(act_ready, 1)

            def take_weights(j):
                dve.wait_ge(S_turned, j + 1)
                v.tensor_copy(S, psum[:, 4, 0:256]).then_inc(S_ready, 1)

            one_hot(0, pos, slice(0, 1))
            steps.link(v.tensor_copy(cnt[:, :], psum[:, 7, 128:128 + NE]))
            for k in range(NK):
                ins = v.tensor_scalar(more[:, k * NE:(k + 1) * NE], cnt[:, :], float((k + 1) * CAP), None, ALU.is_gt)
            steps.link(ins)
            steps.link(v.tensor_reduce(small[:, 54:55], more[:, :], AX.X, ALU.add))
            v.tensor_copy(novt[:, :], small[:, 54:55]).then_inc(nov_ready, 1)

            with dve.Fori(0, NE // UNROLL) as it:
                steps.begin_loop(it, UNROLL)
                for c in range(UNROLL):
                    j = it * UNROLL + c
                    one_hot_weights(j, pos, wgt, bass.ds(j, 1))
                    one_hot(j + 1, pos, bass.ds(j + 1, 1))
                    swiglu(j, it * (UNROLL * EP) + c * EP)
                    take_weights(j)
                steps.end_loop(NE // UNROLL)

            nov = dve.value_load(novt[0:1, 0:1], min_val=0, max_val=NJ)
            with dve.If(nov > 0):
                dve.wait_ge(ov_pe, 1)
                v.tensor_copy(posT, psum[0:NE, 6, 0:T])
                for k in range(NK):
                    ins = v.tensor_scalar(ovF[:, k:k + 1], psum[0:NE, 6, 256:257], float((k + 1) * CAP), None, ALU.is_gt)
                steps.link(ins)
                v.tensor_reduce(ovn, ovF, AX.X, ALU.add).then_inc(ov_dve, 1)
                dve.wait_ge(ov_pe, 2)
                v.tensor_copy(ovo, psum[0:NE, 6, 300:301])
                v.memset(ovE, 0.0)
                steps.link(v.memset(ovK, 0.0))
                for k in range(NK):
                    steps.link(v.tensor_scalar(ovR, count_up[0:NE, 0:NJ], ovo, float(k), ALU.subtract, ALU.is_equal))
                    steps.link(v.tensor_scalar(ovR, ovR, ovF[:, k:k + 1], None, ALU.mult))
                    v.tensor_tensor(ovE, ovE, ovR, ALU.add)
                    steps.link(v.scalar_tensor_tensor(ovK, ovR, float(-CAP * (k + 1)), ovK, ALU.mult, ALU.add))
                v.tensor_copy(small[:, 61:62], small[:, 0:1]).then_inc(ov_dve, 1)
                dve.wait_ge(ov_pe, 3)
                v.tensor_copy(wgtO, psum[:, 6, 352:352 + 2 * NJ].rearrange("p (t j) -> p t j", t=TT))
                v.tensor_copy(posO, psum[:, 6, 352 + 2 * NJ:352 + 4 * NJ].rearrange("p (t j) -> p t j", t=TT))
                v.tensor_copy(eid[:, :], psum[0:1, 6, 320:320 + NJ]).then_inc(ov_dve, 1)
                dve.wait_ge(ov_dve, 3)
                at0 = steps.n
                with dve.Fori(0, nov) as j:
                    steps.begin_loop(j, 1)
                    one_hot(j + (NE + 1), posO, bass.ds(j, 1))
                    one_hot_weights(j + NE, posO, wgtO, bass.ds(j, 1))
                    swiglu(j + NE, j * EP + NE * EP)
                    take_weights(j + NE)
                    steps.base = steps.before
            dve.wait_ge(scattered, nov + (NE + 1))
            for t in range(TT):
                ins = v.tensor_tensor(xres[:, t, :], psum[:, 2 * t:2 * t + 2, :].rearrange("p h n -> p (h n)"), xres[:, t, :], ALU.add)
            ins.then_inc(x2_ready, 1)
            dve.wait_ge(ssq_ready, 6)
            ms(48)
            dve.wait_ge(rstd_ready, 3)
            dve.wait_ge(gfin_in, 16)
            for t in range(TT):
                v.scalar_tensor_tensor(normed[:, t, :], xres[:, t, :], small[:, 52 + t:53 + t], gbc[:, :], ALU.mult,
                                       ALU.mult).then_inc(out_ready, 1)

        @block.gpsimd
        def _(pool):
            g = nc.gpsimd

            def rstd(nth, col):
                pool.wait_ge(ms_ready, nth)
                g.tensor_tensor(small[:, col + 4:col + 6], small[:, col + 2:col + 4],
                                cst[:, C_COL + 1:C_COL + 2].broadcast_to([P, 2]), ALU.pow).then_inc(rstd_ready, 1)

            g.memset(kz, 0.0).then_inc(kz_ready, 1)
            pool.wait_ge(cst_in, 16)
            rstd(1, 0)

            def split_low(n, s, par):
                pool.wait_ge(wH_ready, n * 2 + 1)
                g.tensor_tensor(wL[:, par, 0, :, :], ring[:, s, :].rearrange("p (k n) -> p k n", k=KB)[:, :, 0:P],
                                wH[:, par, 0, :, :].bitcast(F32), ALU.subtract).then_inc(wL0_ready, 1)

            for n in range(3):
                split_low(n, n, n % 2)
            with pool.Fori(0, NKV) as i:
                for c in range(1, 7):
                    split_low(i * 6 + (2 + c), (2 + c) % RING1, c % 2)
                    if c == 2:
                        pool.wait_ge(bank6_read, i + 1)
                        g.tensor_copy(vcur, V[:, :, bass.ds(i * HD, HD)]).then_inc(vcur_ready, 1)
                    if c == 5:
                        pool.wait_ge(zH_ready, i + 1)
                        g.tensor_tensor(zL[:, bass.ds(i * 2, 2), :], ycv, zH[:, bass.ds(i * 2, 2), :].bitcast(F32),
                                        ALU.subtract).then_inc(zL_ready, 1)
            for n in range(NIN + 1, NP1):
                split_low(n, n % RING1, n % 2)
            rstd(2, 6)
            pool.wait_ge(part_ready, 1)
            pool.wait_ge(h2T_turned, 4)
            g.tensor_tensor(normed[:, :, :], normed[:, :, :], h2b[:, 0, :, :], ALU.subtract).then_inc(rest_ready, 1)
            pool.wait_ge(part_ready, 2)
            pool.wait_ge(rest_ready, 1)
            g.tensor_tensor(h2b[:, 2, :, :], normed[:, :, :], h2b[:, 1, :, :], ALU.subtract).then_inc(part_ready, 1)
            rstd(3, 48)


_INS = ["x", "g_mix", "w_in", "b_in", "sinks", "w_conv", "w_attn_o", "w_conv_o", "w_out", "g_ffn", "w_router", "b_router",
        "w_gate", "b_gate", "w_up", "b_up", "w_down", "b_down", "g_final"]


def kernel(**inputs):
    import concourse.bacc as _bacc
    from concourse.bass_utils import run_bass_kernel_spmd as _run

    nc = _bacc.Bacc("TRN2", target_bir_lowering=False, num_devices=1)
    arrays, args = {}, {}
    given = {name: np.ascontiguousarray(inputs[name]) for name in _INS}
    given["constants"] = shape_constants()
    for name, a in given.items():
        arrays[f"in_{name}"] = a
        args[name] = nc.dram_tensor(f"in_{name}", a.shape, mybir.dt.from_np(a.dtype), kind="ExternalInput").ap()
    out = nc.dram_tensor("out_0", (1, T, D), F32, kind="ExternalOutput").ap()
    hybrid_block(nc, args, out)
    r = _run(nc, [arrays], core_ids=[0])
    return r.results[0]["out_0"]
```
